# Optimizing a Trainium2 kernel written in Bass

```python
import math
import jax, jax.numpy as jnp
from jax import lax
import numpy as np

D_MODEL = 1024
BATCH = 1
SEQ = 1024
DEPTH = 2

N_MIXERS = 4
BLOCK = 128
CONV_K = 4
ROPE_THETA = 10000.0
EPS = 1e-6
LN_EPS = 1e-5
DEEPNORM_ALPHA = (2 * DEPTH) ** 0.25
DEEPNORM_BETA = (8 * DEPTH) ** -0.25

GDN_HEADS = 8
GDN_DK = 128
GDN_DV = 128
GDN_CHUNK = 64
GDN_QK = GDN_HEADS * GDN_DK
GDN_V = GDN_HEADS * GDN_DV
GDN_CONV = 2 * GDN_QK + GDN_V
GDN_IN = GDN_CONV + GDN_V + 2 * GDN_HEADS

SWA_HEADS = 16
SWA_KV_HEADS = 2
SWA_HD = 64
SWA_WINDOW = 128
SWA_Q = SWA_HEADS * SWA_HD
SWA_KV = SWA_KV_HEADS * SWA_HD
SWA_IN = SWA_Q + 2 * SWA_KV + SWA_Q

FOX_HEADS = 16
FOX_HD = 64
FOX_W = FOX_HEADS * FOX_HD
FOX_IN = 4 * FOX_W + FOX_HEADS

MLSTM_HEADS = 8
MLSTM_DQK = 64
MLSTM_DV = 128
MLSTM_CHUNK = 64
MLSTM_QKW = MLSTM_HEADS * MLSTM_DQK
MLSTM_V = MLSTM_HEADS * MLSTM_DV
MLSTM_IN = 2 * MLSTM_QKW + 3 * MLSTM_V + 2 * MLSTM_HEADS

kernel_name = "hybrid_interleaved_gdn_swa_fox_mlstm"

def _n_of(kind):
    return (DEPTH - kind + N_MIXERS - 1) // N_MIXERS

def _rmsnorm(x, g):
    xf = x.astype(jnp.float32)
    y = xf * lax.rsqrt(jnp.mean(xf * xf, axis=-1, keepdims=True) + EPS)
    return (y * g.astype(jnp.float32)).astype(x.dtype)

def _layernorm(x, g, b):
    xf = x.astype(jnp.float32)
    mu = jnp.mean(xf, axis=-1, keepdims=True)
    var = jnp.mean(jnp.square(xf - mu), axis=-1, keepdims=True)
    y = (xf - mu) * lax.rsqrt(var + LN_EPS) * g.astype(jnp.float32) + b.astype(jnp.float32)
    return y.astype(x.dtype)

def _l2norm(x):
    return x * lax.rsqrt(jnp.sum(x * x, axis=-1, keepdims=True) + EPS)

def _causal_conv_silu(x, w):
    ch = x.shape[-1]
    y = lax.conv_general_dilated(
        x, w[:, None, :].astype(x.dtype), window_strides=(1,),
        padding=[(CONV_K - 1, 0)], dimension_numbers=("NWC", "WIO", "NWC"),
        feature_group_count=ch)
    return jax.nn.silu(y)

def _rope(x, pos):
    half = x.shape[-1] // 2
    inv = ROPE_THETA ** (-jnp.arange(half, dtype=jnp.float32) / half)
    ang = pos.astype(jnp.float32)[:, None] * inv[None, :]
    cos = jnp.cos(ang)[None, :, None, :]
    sin = jnp.sin(ang)[None, :, None, :]
    xf = x.astype(jnp.float32)
    x1, x2 = xf[..., :half], xf[..., half:]
    return jnp.concatenate([x1 * cos - x2 * sin, x2 * cos + x1 * sin], axis=-1).astype(x.dtype)

def _chunk_heads(t, n, c, h, d):
    return t.astype(jnp.float32).reshape(t.shape[0], n, c, h, d).transpose(0, 3, 1, 2, 4)

def _chunk_gate(g, n, c):
    return g.reshape(g.shape[0], n, c, g.shape[-1]).transpose(0, 3, 1, 2)

def _unchunk(o):
    n, b, h, c, d = o.shape
    return o.transpose(1, 0, 3, 2, 4).reshape(b, n * c, h, d)

def _gated_deltanet(x, w_in, conv_w, a_log, dt_bias, norm_g, w_out):
    f32 = jnp.float32
    bsz, t_len, _ = x.shape
    H, DK, DV, C = GDN_HEADS, GDN_DK, GDN_DV, GDN_CHUNK
    n = t_len // C
    qkv, z, beta_logit, a_logit = jnp.split(
        x @ w_in, [GDN_CONV, GDN_CONV + GDN_V, GDN_CONV + GDN_V + H], axis=-1)
    qkv = _causal_conv_silu(qkv, conv_w)
    q, k, v = jnp.split(qkv, [GDN_QK, 2 * GDN_QK], axis=-1)
    q = _l2norm(_chunk_heads(q, n, C, H, DK)) * DK ** -0.5
    k = _l2norm(_chunk_heads(k, n, C, H, DK))
    v = _chunk_heads(v, n, C, H, DV)
    beta = _chunk_gate(jax.nn.sigmoid(beta_logit.astype(f32)), n, C)
    g = -jnp.exp(a_log.astype(f32)) * jax.nn.softplus(a_logit.astype(f32) + dt_bias.astype(f32))
    gc = jnp.cumsum(_chunk_gate(g, n, C), axis=-1)
    causal = jnp.tril(jnp.ones((C, C), bool))
    strict = jnp.tril(jnp.ones((C, C), bool), -1)
    decay = jnp.exp(jnp.where(causal, gc[..., :, None] - gc[..., None, :], -jnp.inf))
    kb = k * beta[..., None]
    lmat = jnp.where(strict, jnp.einsum("bhnid,bhnjd->bhnij", kb, k) * decay, 0.0)
    rhs = jnp.concatenate([v * beta[..., None], kb * jnp.exp(gc)[..., None]], axis=-1)
    uw = lax.linalg.triangular_solve(lmat, rhs, left_side=True, lower=True, unit_diagonal=True)
    u, w = uw[..., :DV], uw[..., DV:]
    qk = jnp.where(causal, jnp.einsum("bhnid,bhnjd->bhnij", q, k) * decay, 0.0)
    q_dec = q * jnp.exp(gc)[..., None]
    g_last = gc[..., -1]
    k_dec = k * jnp.exp(g_last[..., None] - gc)[..., None]

    def step(state, xs):
        qk_n, q_n, u_n, w_n, kd_n, gl_n = xs
        v_new = u_n - jnp.einsum("bhcd,bhde->bhce", w_n, state)
        o = jnp.einsum("bhcd,bhde->bhce", q_n, state) + jnp.einsum("bhij,bhje->bhie", qk_n, v_new)
        state = state * jnp.exp(gl_n)[..., None, None] + jnp.einsum("bhcd,bhce->bhde", kd_n, v_new)
        return state, o

    xs = tuple(jnp.moveaxis(a, 2, 0) for a in (qk, q_dec, u, w, k_dec, g_last))
    _, o = lax.scan(step, jnp.zeros((bsz, H, DK, DV), f32), xs)
    o = _rmsnorm(_unchunk(o), norm_g).reshape(bsz, t_len, GDN_V)
    o = o * jax.nn.silu(z.astype(f32))
    return o.astype(x.dtype) @ w_out

def _swa_sinks(x, w_in, sinks, w_out, pos):
    f32 = jnp.float32
    bsz, t_len, _ = x.shape
    H, KVH, HD, W = SWA_HEADS, SWA_KV_HEADS, SWA_HD, SWA_WINDOW
    G = H // KVH
    nb = t_len // W
    q, k, v, z = jnp.split(x @ w_in, [SWA_Q, SWA_Q + SWA_KV, SWA_Q + 2 * SWA_KV], axis=-1)
    q = _rope(q.reshape(bsz, t_len, H, HD), pos)
    k = _rope(k.reshape(bsz, t_len, KVH, HD), pos)
    v = v.reshape(bsz, t_len, KVH, HD)
    qb = q.reshape(bsz, nb, W, KVH, G, HD)

    def with_prev(a):
        ab = a.reshape(bsz, nb, W, KVH, HD)
        prev = jnp.pad(ab, ((0, 0), (1, 0), (0, 0), (0, 0), (0, 0)))[:, :-1]
        return jnp.concatenate([prev, ab], axis=2)

    kb, vb = with_prev(k), with_prev(v)
    s = jnp.einsum("bnqhgd,bnkhd->bnhgqk", qb, kb).astype(f32) * HD ** -0.5
    qi = jnp.arange(W)[:, None]
    kj = jnp.arange(2 * W)[None, :]
    rel = qi + W - kj
    blk = jnp.arange(nb)[:, None, None]
    valid = (rel >= 0) & (rel < W) & (blk * W + kj - W >= 0)
    s = jnp.where(valid[None, :, None, None], s, -jnp.inf)
    sink = jnp.broadcast_to(sinks.astype(f32).reshape(KVH, G)[None, None, :, :, None, None],
                            s.shape[:-1] + (1,))
    p = jax.nn.softmax(jnp.concatenate([s, sink], axis=-1), axis=-1)[..., :-1]
    o = jnp.einsum("bnhgqk,bnkhd->bnqhgd", p.astype(vb.dtype), vb).reshape(bsz, t_len, SWA_Q)
    return (o * jax.nn.silu(z)) @ w_out

def _forgetting_attention(x, w_in, f_bias, q_norm_g, k_norm_g, w_out):
    f32 = jnp.float32
    bsz, t_len, _ = x.shape
    H, HD = FOX_HEADS, FOX_HD
    q, k, v, z, f_logit = jnp.split(x @ w_in, [FOX_W, 2 * FOX_W, 3 * FOX_W, 4 * FOX_W], axis=-1)
    q = _rmsnorm(q.reshape(bsz, t_len, H, HD), q_norm_g)
    k = _rmsnorm(k.reshape(bsz, t_len, H, HD), k_norm_g)
    v = v.reshape(bsz, t_len, H, HD)
    log_f = jax.nn.log_sigmoid(f_logit.astype(f32) + f_bias.astype(f32))
    cum = jnp.cumsum(log_f, axis=1).transpose(0, 2, 1)
    scale = HD ** -0.5
    outs = []
    for nblk in range(t_len // BLOCK):
        lo, hi = nblk * BLOCK, (nblk + 1) * BLOCK
        s = jnp.einsum("bqhd,bkhd->bhqk", q[:, lo:hi], k[:, :hi]).astype(f32) * scale
        bias = cum[:, :, lo:hi, None] - cum[:, :, None, :hi]
        mask = jnp.arange(lo, hi)[:, None] >= jnp.arange(hi)[None, :]
        p = jax.nn.softmax(jnp.where(mask, s + bias, -jnp.inf), axis=-1)
        outs.append(jnp.einsum("bhqk,bkhd->bqhd", p.astype(v.dtype), v[:, :hi]))
    o = jnp.concatenate(outs, axis=1).reshape(bsz, t_len, FOX_W)
    return (o * jax.nn.silu(z)) @ w_out

def _mlstm(x, w_in, conv_w, gate_bias, norm_g, w_out):
    f32 = jnp.float32
    bsz, t_len, _ = x.shape
    H, DQK, DV, C = MLSTM_HEADS, MLSTM_DQK, MLSTM_DV, MLSTM_CHUNK
    n = t_len // C
    qk, v, o_logit, z, gates = jnp.split(
        x @ w_in, [2 * MLSTM_QKW, 2 * MLSTM_QKW + MLSTM_V, 2 * MLSTM_QKW + 2 * MLSTM_V,
                   2 * MLSTM_QKW + 3 * MLSTM_V], axis=-1)
    q, k = jnp.split(_causal_conv_silu(qk, conv_w), 2, axis=-1)
    q = _chunk_heads(q, n, C, H, DQK) * DQK ** -0.5
    k = _chunk_heads(k, n, C, H, DQK)
    v = _chunk_heads(v, n, C, H, DV)
    gates = gates.astype(f32) + gate_bias.astype(f32)
    ig = _chunk_gate(gates[..., :H], n, C)
    lf = jax.nn.log_sigmoid(_chunk_gate(gates[..., H:], n, C))
    b = jnp.cumsum(lf, axis=-1)
    causal = jnp.tril(jnp.ones((C, C), bool))
    d_intra = jnp.where(causal, b[..., :, None] - b[..., None, :] + ig[..., None, :], -jnp.inf)
    m_intra = jnp.max(d_intra, axis=-1)
    qk_s = jnp.einsum("bhnid,bhnjd->bhnij", q, k)
    a_end = b[..., -1:] - b + ig
    m_end = jnp.max(a_end, axis=-1)

    def step(carry, xs):
        c_st, n_st, m_st = carry
        q_n, k_n, v_n, d_n, s_n, mi_n, b_n, ae_n, me_n = xs
        inter = b_n + m_st[..., None]
        m_t = jnp.maximum(inter, mi_n)
        p = s_n * jnp.exp(d_n - m_t[..., None])
        w_inter = jnp.exp(inter - m_t)
        num = w_inter[..., None] * jnp.einsum("bhcd,bhde->bhce", q_n, c_st) + jnp.einsum("bhij,bhje->bhie", p, v_n)
        den = w_inter * jnp.einsum("bhcd,bhd->bhc", q_n, n_st) + jnp.sum(p, axis=-1)
        h = num / jnp.maximum(jnp.abs(den), jnp.exp(-m_t))[..., None]
        m_new = jnp.maximum(b_n[..., -1] + m_st, me_n)
        w_old = jnp.exp(b_n[..., -1] + m_st - m_new)
        w_tok = jnp.exp(ae_n - m_new[..., None])
        c_st = w_old[..., None, None] * c_st + jnp.einsum("bhcd,bhce->bhde", k_n * w_tok[..., None], v_n)
        n_st = w_old[..., None] * n_st + jnp.einsum("bhcd,bhc->bhd", k_n, w_tok)
        return (c_st, n_st, m_new), h

    xs = tuple(jnp.moveaxis(a, 2, 0) for a in (q, k, v, d_intra, qk_s, m_intra, b, a_end, m_end))
    init = (jnp.zeros((bsz, H, DQK, DV), f32), jnp.zeros((bsz, H, DQK), f32), jnp.zeros((bsz, H), f32))
    _, h = lax.scan(step, init, xs)
    h = _rmsnorm(_unchunk(h), norm_g).reshape(bsz, t_len, MLSTM_V)
    h = h * jax.nn.sigmoid(o_logit.astype(f32)) * jax.nn.silu(z.astype(f32))
    return h.astype(x.dtype) @ w_out

def setup_inputs(seed: int = 0) -> dict:
    key = jax.random.key(seed)
    ks = iter(jax.random.split(key, 32))

    def nrm(shape, scale):
        return scale * jax.random.normal(next(ks), shape, jnp.float32)

    na, nb, nc, nd = (_n_of(m) for m in range(N_MIXERS))
    x = nrm((BATCH, SEQ, D_MODEL), 1.0)
    a_w_in = nrm((na, D_MODEL, GDN_IN), D_MODEL ** -0.5)
    a_conv = nrm((na, CONV_K, GDN_CONV), CONV_K ** -0.5)
    a_a_log = jnp.log(jax.random.uniform(next(ks), (na, GDN_HEADS), jnp.float32, 1.0, 16.0))
    dt = jnp.exp(jax.random.uniform(next(ks), (na, GDN_HEADS), jnp.float32, math.log(1e-3), math.log(1e-1)))
    a_dt_bias = dt + jnp.log(-jnp.expm1(-dt))
    a_norm_g = 1.0 + nrm((na, GDN_DV), 0.02)
    a_w_out = nrm((na, GDN_V, D_MODEL), GDN_V ** -0.5 * DEEPNORM_BETA)
    b_w_in = nrm((nb, D_MODEL, SWA_IN), D_MODEL ** -0.5)
    b_sinks = nrm((nb, SWA_HEADS), 0.5)
    b_w_out = nrm((nb, SWA_Q, D_MODEL), SWA_Q ** -0.5 * DEEPNORM_BETA)
    c_w_in = nrm((nc, D_MODEL, FOX_IN), D_MODEL ** -0.5)
    c_f_bias = 2.0 + nrm((nc, FOX_HEADS), 0.5)
    c_q_norm = 1.0 + nrm((nc, FOX_HD), 0.02)
    c_k_norm = 1.0 + nrm((nc, FOX_HD), 0.02)
    c_w_out = nrm((nc, FOX_W, D_MODEL), FOX_W ** -0.5 * DEEPNORM_BETA)
    d_w_in = nrm((nd, D_MODEL, MLSTM_IN), D_MODEL ** -0.5)
    d_conv = nrm((nd, CONV_K, 2 * MLSTM_QKW), CONV_K ** -0.5)
    d_gate_bias = jnp.concatenate([nrm((nd, MLSTM_HEADS), 0.1), 3.0 + nrm((nd, MLSTM_HEADS), 0.5)], axis=-1)
    d_norm_g = 1.0 + nrm((nd, MLSTM_DV), 0.02)
    d_w_out = nrm((nd, MLSTM_V, D_MODEL), MLSTM_V ** -0.5 * DEEPNORM_BETA)
    ln_g = 1.0 + nrm((DEPTH, D_MODEL), 0.02)
    ln_b = nrm((DEPTH, D_MODEL), 0.02)
    return {"x": x,
            "a_w_in": a_w_in, "a_conv": a_conv, "a_a_log": a_a_log, "a_dt_bias": a_dt_bias,
            "a_norm_g": a_norm_g, "a_w_out": a_w_out,
            "b_w_in": b_w_in, "b_sinks": b_sinks, "b_w_out": b_w_out,
            "c_w_in": c_w_in, "c_f_bias": c_f_bias, "c_q_norm": c_q_norm, "c_k_norm": c_k_norm,
            "c_w_out": c_w_out,
            "d_w_in": d_w_in, "d_conv": d_conv, "d_gate_bias": d_gate_bias, "d_norm_g": d_norm_g,
            "d_w_out": d_w_out,
            "ln_g": ln_g, "ln_b": ln_b}

def reference(x, a_w_in, a_conv, a_a_log, a_dt_bias, a_norm_g, a_w_out,
              b_w_in, b_sinks, b_w_out,
              c_w_in, c_f_bias, c_q_norm, c_k_norm, c_w_out,
              d_w_in, d_conv, d_gate_bias, d_norm_g, d_w_out,
              ln_g, ln_b):
    pos = jnp.arange(x.shape[1], dtype=jnp.int32)
    for i in range(DEPTH):
        kind, j = i % N_MIXERS, i // N_MIXERS
        if kind == 0:
            y = _gated_deltanet(x, a_w_in[j], a_conv[j], a_a_log[j], a_dt_bias[j], a_norm_g[j], a_w_out[j])
        elif kind == 1:
            y = _swa_sinks(x, b_w_in[j], b_sinks[j], b_w_out[j], pos)
        elif kind == 2:
            y = _forgetting_attention(x, c_w_in[j], c_f_bias[j], c_q_norm[j], c_k_norm[j], c_w_out[j])
        else:
            y = _mlstm(x, d_w_in[j], d_conv[j], d_gate_bias[j], d_norm_g[j], d_w_out[j])
        x = _layernorm(DEEPNORM_ALPHA * x + y, ln_g[i], ln_b[i])
    return x


_drawn_inputs = setup_inputs


def setup_inputs(seed=0):
    import zlib

    import numpy as np

    out = dict(_drawn_inputs(seed))
    spreads = {}
    factors = {'a_norm_g': 23.321, 'b_sinks': 33.478}
    for name, (base, spread) in spreads.items():
        noise = np.random.default_rng([zlib.crc32(name.encode()), seed]).standard_normal(out[name].shape)
        drawn = base * np.exp(spread * noise) if base else spread * noise
        out[name] = __import__('jax').numpy.asarray(drawn.astype(out[name].dtype))
    for name, factor in factors.items():
        out[name] = (out[name] * factor).astype(out[name].dtype)
    return out
```

```python
from contextlib import ExitStack

import numpy as np

import concourse.bass as bass
from concourse import mybir

F32 = mybir.dt.float32
F32R = mybir.dt.float32r
ALU = mybir.AluOpType
ACT = mybir.ActivationFunctionType

P = 128
SEQ = 1024
DM = 1024
NT = SEQ // P
NK = DM // P
HALF = 512
ALPHA = float(4 ** 0.25)
EPS = 1e-6
LN_EPS = 1e-5
NEG = -1e30

GH = 8
CONV_K = 4
QKV_TILES = 3 * GH
TILES = QKV_TILES + GH
GDN_IN = 4112
GATE_COL = 128 * TILES
QKV_GROUPS = 2 * QKV_TILES

SH = 16
HD = 64
KVH = 2
SWA_Z0 = 1280
SCALE = HD ** -0.5
UNITS = SH // 4 * NT
WR = 10
SLICES = 3 * NK

PASSES = 3
GROUP = NK * PASSES
STEP = 3


AT_ROOTS, AT_SCALE, AT_OUT = 0.175, 0.185, 0.2
AT_TOKEN = (0.215, 0.25)
AT_MATRIX, AT_MATRIX_STEP = 0.29, 0.02
AT_BLOCKS, AT_INVERSE, AT_INVERSE_STEP = 0.4, 0.465, 0.02
AT_SCAN, AT_SCAN_STEP = 0.54, 0.026
LAST_BLOCKS, LAST_INVERSE, LAST_SCAN, LAST_SCAN_STEP = 0.21, 0.23, 0.32, 0.028


def plan(p):
    if p < GH:
        groups = list(range(6 * p, 6 * p + 6))
    elif p < GH + 2:
        groups = list(range(QKV_GROUPS + GH * (p - GH), QKV_GROUPS + GH * (p - GH + 1)))
    else:
        groups = []
    last = 2 * TILES - 2
    events = []
    for i, g in enumerate(groups):
        t0 = GROUP * i
        for q in range(0, GROUP, STEP):
            events.append((t0 + q, 0, ("mm", g, q)))
        end = t0 + GROUP - 0.5
        events.append((end, 1, ("end", g, 0)))
        if g % 2 == 0 and g // 2 + 1 < TILES:
            events.append((t0 + 4, 1, ("weights", g // 2 + 1, 0)))
            if g // 2 + 2 < TILES:
                events.append((t0 + 16, 1, ("fetch", g // 2 + 2, 0)))
        if g % 2 == 0 and g // 2 + 1 < TILES:
            events.append((t0 + 9, 1, ("low", g // 2 + 1, 0)))
        for k in range(5 if g < QKV_GROUPS else 2):
            if g < last:
                events.append((end + 0.2 + k * 4.2, 2, ("piece", g, k)))
            elif k == 0:
                events.append((end + 0.2, 2, ("piece", g, k)))
    span = GROUP * max(len(groups), 1)
    slots = []
    if 0 <= p - 3 < GH or 0 <= p - 2 < GH:
        slots += [(AT_ROOTS, ("OF", 0))]
    if 0 <= p - 3 < GH:
        slots += [(AT_SCALE, ("OS", 0)), (AT_OUT, ("OT", 0))]
    if 0 <= p - 2 < GH:
        slots += [(AT_SCALE, ("VS", 0))]
    if 0 <= p - 1 < GH:
        slots += [(AT_TOKEN[i], ("T", i)) for i in range(2)]
        slots += [(AT_MATRIX + AT_MATRIX_STEP * c, ("M", c)) for c in range(NT + 1)]
    for r in (p - 3, p - 2):
        if 0 <= r < GH:
            blocks, inverse, scan, step = (AT_BLOCKS, AT_INVERSE, AT_SCAN, AT_SCAN_STEP) if r < GH - 1 else \
                                          (LAST_BLOCKS, LAST_INVERSE, LAST_SCAN, LAST_SCAN_STEP)
            items = [(blocks, ("X", 0))] + [(inverse + AT_INVERSE_STEP * i, ("L", i)) for i in range(4)]
            items += [(scan + step * (3 * c + i), ("ABC"[i], c)) for c in range(NT) for i in range(3)]
            shift = p - 2 - r
            slots += [(at - shift, (n, c, r)) for at, (n, c) in items if 0 <= at - shift < 1]
    for at, item in slots:
        events.append((at * span, 3, (item + (0,))[:3]))
    events.sort(key=lambda e: (e[0], e[1]))
    out = [e[2] for e in events]
    if p == GH + 2:
        out += [("piece", last, 1), ("piece", last + 1, 1)]
    return out


PLANS = [plan(p) for p in range(GH + 3)]


class Link:

    def __init__(self, eng, sem):
        self.eng, self.sem, self.n = eng, sem, 0

    def next(self, ins):
        ins.then_inc(self.sem, 1)
        self.n += 1

    def wait(self):
        self.eng.wait_ge(self.sem, self.n)


def hybrid_trunk(nc, x, a_w_in, a_conv, a_a_log, a_dt_bias, a_norm_g, a_w_out, b_w_in, b_sinks, b_w_out,
                 ln_g, ln_b, rope_cos, rope_sin, out, stop=None):
    wa = a_w_in[0]
    wb = b_w_in[0]
    w_out = [a_w_out[0], b_w_out[0]]
    blocks_in = nc.dram_tensor("blocks_in", [2, NT * 4, 32, 32], F32).ap()
    blocks_out = nc.dram_tensor("blocks_out", [2, NT * 4, 32, 32], F32).ap()
    ctx = ExitStack()
    with ctx:
        def sem(name):
            return ctx.enter_context(nc.semaphore(name))

        def sbuf(stack, name, shape, dt=F32):
            return stack.enter_context(nc.sbuf_tensor(name, shape, dt))

        ps = ctx.enter_context(nc.psum_tensor("ps", [P, 8, HALF], F32))

        act_hi = sbuf(ctx, "act_hi", [P, NK, SEQ], F32R)
        act_lo = sbuf(ctx, "act_lo", [P, NK, SEQ], F32R)
        tok = sbuf(ctx, "tok", [P, NT, SEQ])
        ident = sbuf(ctx, "ident", [P, P])

        st = ExitStack()
        qT = [sbuf(st, f"qT{i}", [P, SEQ]) for i in range(3)]
        kT = [sbuf(st, f"kT{i}", [P, SEQ]) for i in range(3)]
        vT = sbuf(st, "vT", [P, SEQ])
        k_dec = [sbuf(st, f"k_dec{i}", [P, NT, P]) for i in range(2)]
        v_tok = [sbuf(st, f"v_tok{i}", [P, NT, P]) for i in range(2)]
        aT = [sbuf(st, f"aT{i}", [P, NT, P]) for i in range(2)]
        nT = [sbuf(st, f"nT{i}", [P, NT, P]) for i in range(2)]
        xT = sbuf(st, "xT", [P, NT, P])
        o_tok = sbuf(st, "o_tok", [P, NT, P])
        o_flat = o_tok[:, :, :].rearrange("p a b -> p (a b)")
        xr = o_flat[:, 0:NT * 64].rearrange("p (c j) -> p c j", c=NT)
        uT = o_flat[:, NT * 64:NT * 128].rearrange("p (c j) -> p c j", c=NT)
        w_raw = sbuf(st, "w_raw", [P, NK, P])
        w_hi = [sbuf(st, f"w_hi{i}", [P, NK, P], F32R) for i in range(2)]
        w_lo = [sbuf(st, f"w_lo{i}", [P, NK, P], F32R) for i in range(2)]
        xs = sbuf(st, "xs", [P, 2, HALF + CONV_K - 1])
        conv = sbuf(st, "conv", [P, HALF])
        th = sbuf(st, "th", [P, HALF])
        state = sbuf(st, "state", [P, P])
        resid = sbuf(st, "resid", [P, P])
        q_state = sbuf(st, "q_state", [P, P])
        v_new = sbuf(st, "v_new", [P, P])
        decay = [sbuf(st, f"decay{i}", [P, P]) for i in range(2)]
        blocks = sbuf(st, "blocks", [32, 32, 32])
        rank1 = sbuf(st, "rank1", [32, 256])
        tri = sbuf(st, "tri", [P, P])
        causal = sbuf(st, "causal", [P, P])
        sc = {n: sbuf(st, "sc_" + n, [P, GH, NT]) for n in
              ("beta", "g", "gc", "exp", "nexp", "kdec", "elast", "ssk", "ssq", "cj", "ncj", "rk", "aq", "sso")}
        bias2 = sbuf(st, "bias2", [P, 2, GH])
        convw = sbuf(st, "convw", [P, CONV_K, QKV_TILES])
        norm_g = sbuf(st, "norm_g", [P, 1])
        sq_junk = sbuf(st, "sq_junk", [P, 2, P])
        sso_junk = sbuf(st, "sso_junk", [P, 2, P])
        gates = vT[0:16, :]
        conv_rows = qT[0][0:CONV_K, :]
        gt = conv[:, :].rearrange("p (a h c) -> p a h c", a=8, h=GH)
        st.close()

        st = ExitStack()
        bT = sbuf(st, "bT", [P, NK, SEQ])
        st1 = ExitStack()
        kd = sbuf(st1, "kd", [P, 2, P + SEQ])
        vv = sbuf(st1, "vv", [P, 1 + NT, P])
        window = sbuf(st1, "window", [P, 2, 2 * P])
        sinks = sbuf(st1, "sinks", [P, SH])
        stp = ExitStack()
        ws_raw = sbuf(stp, "ws_raw", [P, 2, HALF])
        ws_hi = sbuf(stp, "ws_hi", [P, WR, HALF], F32R)
        ws_lo = sbuf(stp, "ws_lo", [P, WR, HALF], F32R)
        cosr = sbuf(stp, "cosr", [P, NT, HD])
        sinr = sbuf(stp, "sinr", [P, NT, HD])
        rot = sbuf(stp, "rot", [P, 2, HALF])
        qr = sbuf(stp, "qr", [P, 2, HALF])
        stp.close()
        stz = ExitStack()
        z_raw = sbuf(stz, "z_raw", [P, NK, P])
        z_hi = [sbuf(stz, f"z_hi{i}", [P, NK, P], F32R) for i in range(2)]
        z_lo = [sbuf(stz, f"z_lo{i}", [P, NK, P], F32R) for i in range(2)]
        zg = sbuf(stz, "zg", [P, 2, SEQ])
        zt = sbuf(stz, "zt", [P, HALF])
        logit = sbuf(stz, "logit", [P, 2, 4, 2 * P])
        prob = sbuf(stz, "prob", [P, 2, 2, 4, P])
        sm = {n: sbuf(stz, "sm_" + n, [P, 2, 4]) for n in ("max", "neg", "sum", "off", "sink", "den", "rden")}
        stz.close()
        st1.close()
        st.close()

        st = ExitStack()
        lng = sbuf(st, "lng", [P, DM])
        lnb = sbuf(st, "lnb", [P, DM])
        xres = sbuf(st, "xres", [P, 2, DM])
        yr = sbuf(st, "yr", [P, 2, DM])
        fill = sbuf(st, "fill", [P, 2 * DM])
        stats = sbuf(st, "stats", [P, 2, 2, 6])
        mv = sbuf(st, "mv", [P, 2, 4])
        wo_raw = sbuf(st, "wo_raw", [P, 2, DM])
        wo_hi = sbuf(st, "wo_hi", [P, NK, DM], F32R)
        wo_lo = sbuf(st, "wo_lo", [P, NK, DM], F32R)
        st.close()

        s_const = sem("s_const")
        s_x = [sem(f"s_x{t}") for t in range(NT)]
        s_small = sem("s_small")
        s_xtr = sem("s_xtr")
        s_xhi = sem("s_xhi")
        s_xlo = sem("s_xlo")
        s_ctr = sem("s_ctr")
        s_cw = sem("s_cw")
        s_wraw = sem("s_wraw")
        s_whi = sem("s_whi")
        s_wlo = sem("s_wlo")
        s_group = sem("s_group")
        s_gev = sem("s_gev")
        s_gtr = sem("s_gtr")
        s_gd = sem("s_gd")
        s_ga = sem("s_ga")
        s_gc = sem("s_gc")
        s_halo = sem("s_halo")
        s_evac = sem("s_evac")
        s_tap = sem("s_tap")
        s_th = sem("s_th")
        s_silu = sem("s_silu")
        s_zth = sem("s_zth")
        s_zt = sem("s_zt")
        s_gated = sem("s_gated")
        s_kd = sem("s_kd")
        s_dve = sem("s_dve")
        s_act = sem("s_act")
        s_tr = sem("s_tr")
        s_sq = sem("s_sq")
        s_sk = sem("s_sk")
        s_tev = sem("s_tev")
        s_ak = sem("s_ak")
        s_rk = sem("s_rk")
        s_vs = sem("s_vs")
        s_gcr = sem("s_gcr")
        s_dp = sem("s_dp")
        s_dt = sem("s_dt")
        s_kk = sem("s_kk")
        s_m = sem("s_m")
        s_pin = sem("s_pin")
        s_pb = sem("s_pb")
        s_pool = sem("s_pool")
        s_inv = sem("s_inv")
        s_pout = sem("s_pout")
        s_xt = sem("s_xt")
        s_xr = sem("s_xr")
        s_lv = sem("s_lv")
        s_ut = sem("s_ut")
        s_xl = sem("s_xl")
        s_ks = sem("s_ks")
        s_qs = sem("s_qs")
        s_resid = sem("s_resid")
        s_oq = sem("s_oq")
        s_y = sem("s_y")
        s_vnew = sem("s_vnew")
        s_su = sem("s_su")
        s_av = sem("s_av")
        s_state = sem("s_state")
        s_o = sem("s_o")
        s_sso = sem("s_sso")
        s_of = sem("s_of")
        s_fs = sem("s_fs")
        s_oscaled = sem("s_oscaled")
        s_ot = sem("s_ot")
        s_otev = sem("s_otev")

        s_out = sem("s_out")
        L = []
        for i in range(2):
            L.append({n: sem(f"l{i}_{n}") for n in
                      ("ohi", "olo", "woraw", "wohi", "wolo", "y", "params", "yev", "st", "sqrt", "dve", "ln",
                       "xtr", "xhi", "xlo")})
            L[i]["x"] = [sem(f"l{i}_x{j}") for j in range(2)]
            L[i]["o"] = [sem(f"l{i}_o{j}") for j in range(2)]
            L[i]["wr"] = [sem(f"l{i}_wr{j}") for j in range(2)]

        q_c = sem("q_const")
        q_small = sem("q_small")
        q_raw = [sem(f"q_raw{i}") for i in range(2)]
        q_hi = sem("q_hi")
        q_lo = sem("q_lo")
        q_group = sem("q_group")
        q_rope = sem("q_rope")
        q_dve = sem("q_dve")
        q_tr = sem("q_tr")
        q_tev = sem("q_tev")
        z_rawd = sem("z_rawd")
        z_his = sem("z_his")
        z_los = sem("z_los")
        z_group = sem("z_group")
        z_th = sem("z_th")
        z_t = sem("z_t")
        s_s = sem("s_s")
        s_logit = sem("s_logit")
        s_neg = sem("s_neg")
        s_e = sem("s_e")
        s_norm = sem("s_norm")
        s_pt = sem("s_pt")
        s_pe0 = sem("s_pe0")
        s_pe1 = sem("s_pe1")
        s_pv = sem("s_pv")
        s_ob = sem("s_ob")
        s_bg = sem("s_bg")

        wa_tiles = wa.rearrange("(k p) n -> p k n", p=P)
        wb_tiles = wb.rearrange("(k p) n -> p k n", p=P)
        block = ctx.enter_context(nc.Block())

        def bank_free(eng, g):
            if g < 0:
                eng.wait_ge(s_gev, g + 3)
            elif g < QKV_GROUPS:
                eng.wait_ge(s_evac, g + 1)
            else:
                eng.wait_ge(s_zt, g - QKV_GROUPS + 1)

        def channel_tile(w):
            return (w % 3) * GH + w // 3 if w < QKV_TILES else w

        @block.sync
        def _(sp):
            for t in range(NT):
                sp.dma_start(tok[:, t, :], x[0, t * P:(t + 1) * P, :]).then_inc(s_x[t], 16)
            sp.dma_start(bias2[:, 0, :], a_dt_bias[0].partition_broadcast(P)).then_inc(s_small, 16)
            sp.dma_start(bias2[:, 1, :], a_a_log[0].partition_broadcast(P)).then_inc(s_small, 16)
            sp.dma_start(norm_g[:, :], a_norm_g[0].rearrange("(p a) -> p a", a=1)).then_inc(s_small, 16)
            for i, buf in enumerate((qT[0], kT[0], qT[1])):
                sp.dma_start(buf[0:CONV_K, :], a_conv[0][:, DM * i:DM * (i + 1)]).then_inc(s_small, 16)
            for h in range(GH):
                sp.wait_ge(s_m, NT * (h + 1))
                for b in range(4):
                    sp.dma_start(blocks_in[h % 2].rearrange("(c b) j i -> b j c i", b=4)[b],
                                 nT[h % 2][32 * b:32 * b + 32, :, 32 * b:32 * b + 32]).then_inc(s_pin, 16)
                sp.wait_ge(s_pin, 64 * (h + 1))
                sp.dma_start(blocks[:, :, :], blocks_in[h % 2]).then_inc(s_pb, 16)
                sp.wait_ge(s_inv, h + 1)
                sp.dma_start(blocks_out[h % 2], blocks[:, :, :]).then_inc(s_pout, 16)
                sp.wait_ge(s_pout, 16 * (h + 1))
                if h:
                    sp.wait_ge(s_y, NT * h)
                else:
                    sp.wait_ge(s_const, 12)
                for b in range(4):
                    sp.dma_start(xT[32 * b:32 * b + 32, :, 32 * b:32 * b + 32],
                                 blocks_out[h % 2].rearrange("(c b) j i -> b j c i", b=4)[b]).then_inc(s_xt, 16)

            def out_stage(i):
                s = L[i]
                if i == 0:
                    sp.wait_ge(s_gated, 2 * GH)
                else:
                    sp.wait_ge(s_bg, NK)
                for k in range(NK):
                    if k >= 2:
                        sp.wait_ge(s["wolo"], k - 1)
                    sp.dma_start(wo_raw[:, k % 2, :], w_out[i][k * P:(k + 1) * P, :]).then_inc(s["wr"][k % 2], 16)
                sp.wait_ge(s["olo"], NK)
                sp.dma_start(lng[:, :], ln_g[i].partition_broadcast(P)).then_inc(s["params"], 16)
                sp.dma_start(lnb[:, :], ln_b[i].partition_broadcast(P)).then_inc(s["params"], 16)
                for t in range(NT):
                    if i == 0:
                        if t >= 2:
                            sp.wait_ge(s["yev"], 2 * (t - 1))
                        sp.dma_start(xres[:, t % 2, :], x[0, t * P:(t + 1) * P, :]).then_inc(s["x"][t % 2], 16)
                    else:
                        sp.wait_ge(s["ln"], t + 1)
                        sp.dma_start(out[0, t * P:(t + 1) * P, :], yr[:, t % 2, :]).then_inc(s["o"][t % 2], 16)

            out_stage(0)
            if stop == 0:
                sp.wait_ge(L[0]["ln"], NT)
                sp.dma_start(out[0].rearrange("(t p) n -> p t n", p=P), tok[:, :, :]).then_inc(s_out, 16)
                sp.wait_ge(s_out, 16)
                return
            sp.wait_ge(L[0]["xlo"], 2 * NT)
            sp.dma_start(cosr[:, :, :], rope_cos.rearrange("(t p) d -> p t d", p=P)).then_inc(q_small, 16)
            sp.dma_start(sinr[:, :, :], rope_sin.rearrange("(t p) d -> p t d", p=P)).then_inc(q_small, 16)
            sp.dma_start(sinks[:, :], b_sinks[0].partition_broadcast(P)).then_inc(q_small, 16)
            for n in range(SLICES):
                if n >= 2:
                    sp.wait_ge(q_lo, n - 1)
                bl, k = n // NK, n % NK
                c0, w = ((DM, 256), (0, HALF), (HALF, HALF))[bl]
                sp.dma_start(ws_raw[:, n % 2, 0:w], wb[k * P:(k + 1) * P, c0:c0 + w]).then_inc(q_raw[n % 2], 16)
            sp.wait_ge(q_tev, 3 * NT)
            for j in range(NK):
                if j:
                    sp.wait_ge(z_los, j)
                sp.dma_start(z_raw[:, :, :], wb_tiles[:, :, SWA_Z0 + P * j:SWA_Z0 + P * (j + 1)]).then_inc(z_rawd, 16)
            out_stage(1)
            for j in range(2):
                sp.wait_ge(L[1]["o"][j], 16 * NT // 2)

        @block.gpsimd
        def _(pool):
            steps = Link(pool, s_const)
            steps.next(pool.memset(ident[:, :], 0.0))
            steps.next(pool.memset(tri[:, :], 1.0))
            steps.next(pool.memset(causal[:, :], 0.0))
            steps.next(pool.memset(w_raw[:, :, 16:P], 0.0))
            steps.next(pool.memset(xs[:, 0, 0:CONV_K - 1], 0.0))
            steps.wait()
            steps.next(pool.affine_select(out=ident[:, :], in_=ident[:, :], compare_op=ALU.not_equal, fill=1.0,
                                          base=0, pattern=[[-1, P]], channel_multiplier=1))
            steps.next(pool.affine_select(out=tri[:, :], in_=tri[:, :], compare_op=ALU.is_ge, fill=0.0,
                                          base=0, pattern=[[1, P]], channel_multiplier=-1))
            steps.next(pool.affine_select(out=causal[:, :], in_=causal[:, :], compare_op=ALU.is_ge, fill=NEG,
                                          base=0, pattern=[[1, P]], channel_multiplier=-1))
            for q in range(4):
                steps.next(pool.memset(xT[:, 2 * q:2 * q + 2, :], 0.0))
            inner = Link(pool, s_pool)
            for h in range(GH):
                pool.wait_ge(s_pb, 16 * (h + 1))
                for m in range(30, 0, -1):
                    w = 31 - m
                    part = rank1[:, 0:m * w].rearrange("p (a b) -> p a b", a=m)
                    inner.next(pool.tensor_tensor(part, blocks[:, 0:m, m:m + 1].broadcast_to([32, m, w]),
                                                  blocks[:, m:m + 1, m + 1:32].broadcast_to([32, m, w]), ALU.mult))
                    inner.wait()
                    inner.next(pool.tensor_tensor(blocks[:, 0:m, m + 1:32], blocks[:, 0:m, m + 1:32], part, ALU.add))
                    inner.wait()
                flat = blocks[:, :, :].rearrange("p a b -> p (a b)")
                pool.memset(flat[:, 0:1024:33], 1.0).then_inc(s_inv, 1)
            if stop == 0:
                return
            pool.wait_ge(L[0]["xlo"], 2 * NT)
            steps = Link(pool, q_c)
            steps.next(pool.memset(kd[:, :, 0:P], 0.0))
            steps.next(pool.memset(vv[:, 0, :], 0.0))
            steps.next(pool.memset(window[:, :, :], 0.0))
            steps.wait()
            steps.next(pool.affine_select(out=window[:, :, :], in_=window[:, :, :], compare_op=ALU.is_gt, fill=NEG,
                                          base=0, pattern=[[0, 2], [1, 2 * P]], channel_multiplier=-1))
            steps.wait()
            steps.next(pool.affine_select(out=window[:, :, :], in_=window[:, :, :], compare_op=ALU.is_ge, fill=NEG,
                                          base=P, pattern=[[0, 2], [-1, 2 * P]], channel_multiplier=1))
            steps.wait()
            steps.next(pool.memset(window[:, 0, 0:P], NEG))

        @block.tensor
        def _(pe):
            pe.wait_ge(s_const, 8)
            for t in range(NT):
                pe.wait_ge(s_x[t], 16)
                for b in range(2):
                    n = 2 * t + b
                    if n >= 4:
                        pe.wait_ge(s_xlo, n - 3)
                    for k in range(4):
                        mm = pe.transpose(ps[:, 4 + n % 4, k * P:(k + 1) * P],
                                          tok[:, t, (4 * b + k) * P:(4 * b + k + 1) * P], ident[:, :])
                    mm.then_inc(s_xtr, 1)
            pe.wait_ge(s_small, 96)
            for w in range(QKV_TILES):
                buf = (qT[0], kT[0], qT[1])[w // 8]
                mm = pe.transpose(ps[:, 2, CONV_K * w:CONV_K * (w + 1)], buf[0:CONV_K, (w % 8) * P:(w % 8 + 1) * P],
                                  ident[0:CONV_K, 0:CONV_K])
            mm.then_inc(s_ctr, 1)
            pe.wait_ge(s_xlo, 2 * NT)

            def project(g, q):
                w, b = g // 2, g % 2
                if q == 0:
                    pe.wait_ge(s_whi, w + 2)
                    pe.wait_ge(s_wlo, w + 2)
                    if g >= 0:
                        bank_free(pe, g - 2)
                for i in range(q, q + STEP):
                    k, j = i // PASSES, i % PASSES
                    lhs = (w_hi, w_hi, w_lo)[j][w % 2]
                    rhs = (act_hi, act_lo, act_hi)[j]
                    mm = pe.matmul(ps[:, g % 2, :], lhs[:, k, :], rhs[:, k, HALF * b:HALF * (b + 1)],
                                   start=(i == 0), stop=(i == GROUP - 1))
                if q + STEP == GROUP:
                    mm.then_inc(s_group, 1)

            for g in (-2, -1):
                for q in range(0, GROUP, STEP):
                    project(g, q)
            pe.wait_ge(s_gev, 2)
            for c in range(NT):
                mm = pe.transpose(ps[:, 3, 16 * c:16 * (c + 1)], gates[:, c * P:(c + 1) * P], ident[0:16, 0:16])
            mm.then_inc(s_gtr, 1)
            pe.wait_ge(s_gd, 3)
            g_all = sc["g"][:, :, :].rearrange("p h c -> p (h c)")
            pe.matmul(ps[:, 3, 128:192], tri[:, :], g_all, start=True, stop=True)
            pe.matmul(ps[:, 3, 192:256], tri[:, P - 1:P].broadcast_to([P, P]), g_all,
                      start=True, stop=True).then_inc(s_gc, 1)

            def token_major(h, i):
                if i == 0:
                    pe.wait_ge(s_silu, 6 * (h + 1))
                    if h >= 1:
                        pe.wait_ge(s_m, NT * h)
                    if h >= 2:
                        pe.wait_ge(s_xl, 2 * (h - 1))
                        pe.wait_ge(s_otev, 2 * (h - 1))
                if 2 * h + i > 0:
                    pe.wait_ge(s_tev, 2 * h + i)
                    pe.wait_ge(s_sk, 4 * (2 * h + i))
                for bank, src in ((6, qT[h % 3]), (7, kT[h % 3]), (5, vT)):
                    for c in range(4):
                        mm = pe.transpose(ps[:, bank, c * P:(c + 1) * P],
                                          src[:, (4 * i + c) * P:(4 * i + c + 1) * P], ident[:, :])
                mm.then_inc(s_tr, 1)

            def scores(h, c):
                if c == 0:
                    pe.wait_ge(s_tev, 2 * h + 2)
                    pe.wait_ge(s_sk, NT * (h + 1))
                else:
                    pe.wait_ge(s_dp, NT * h + c)
                pe.matmul(ps[:, 7, 0:P], sc["g"][:, h, c:c + 1].broadcast_to([P, P]), tri[:, :],
                          start=True, stop=True).then_inc(s_gcr, 1)
                if c >= 2:
                    pe.wait_ge(s_m, NT * h + c - 1)
                bank = 5 + c % 2
                cut = slice(c * P, (c + 1) * P)
                pe.matmul(ps[:, bank, 0:P], kT[h % 3][:, cut], kT[h % 3][:, cut], start=True, stop=True)
                pe.matmul(ps[:, bank, P:2 * P], kT[h % 3][:, cut], qT[h % 3][:, cut],
                          start=True, stop=True).then_inc(s_kk, 1)

            def level(h, i):
                n = nT[h % 2]
                if i == 0:
                    pe.wait_ge(s_xr, h + 1)
                    pe.wait_ge(s_m, NT * min(h + 2, GH))
                    if h >= 1:
                        pe.wait_ge(s_otev, 2 * h)
                elif i == 1:
                    pe.wait_ge(s_ut, 2 * h + 1)
                elif i == 2:
                    pe.wait_ge(s_xl, 2 * h + 1)
                else:
                    pe.wait_ge(s_ut, 2 * h + 2)
                for c in range(NT):
                    if i == 0:
                        for a in (0, 64):
                            b = a + 32
                            mm = pe.matmul(ps[b:b + 32, 6, 32 * c:32 * c + 32], n[a:a + 32, c, b:b + 32],
                                           xr[a:a + 32, c, 0:32], start=True, stop=True)
                    elif i == 1:
                        for a in (0, 64):
                            b = a + 32
                            mm = pe.matmul(ps[a:a + 32, 7, 32 * c:32 * c + 32], uT[b:b + 32, c, 0:32],
                                           xT[b:b + 32, c, b:b + 32], start=True, stop=True)
                        mm = pe.matmul(ps[32:64, 7, 32 * c:32 * c + 32], xT[32:64, c, 32:64], uT[32:64, c, 0:32],
                                       start=True, stop=True)
                    elif i == 2:
                        mm = pe.matmul(ps[64:128, 6, 64 * c:64 * c + 64], n[0:64, c, 64:128], xr[0:64, c, 0:64],
                                       start=True, stop=True)
                    else:
                        mm = pe.matmul(ps[0:64, 7, 64 * c:64 * c + 64], uT[64:128, c, 0:64], xT[64:128, c, 64:128],
                                       start=True, stop=True)
                mm.then_inc(s_lv, 1)

            def with_state(h, c):
                if c == 0:
                    return
                cut = slice(c * P, (c + 1) * P)
                pe.wait_ge(s_state, 7 * h + c)
                pe.wait_ge(s_o, NT * h + c)
                pe.matmul(ps[:, 2, 0:P], kT[h % 3][:, cut], state[:, :], start=True, stop=True).then_inc(s_ks, 1)
                if 7 * h + c - 1 > 0:
                    pe.wait_ge(s_oq, 7 * h + c - 1)
                pe.matmul(ps[:, 3, 0:P], qT[h % 3][:, cut], state[:, :], start=True, stop=True).then_inc(s_qs, 1)

            def solve(h, c):
                if c == 0:
                    pe.wait_ge(s_xl, 2 * h + 2)
                    pe.wait_ge(s_vs, h + 1)
                    rhs = v_tok[h % 2][:, 0, :]
                else:
                    pe.wait_ge(s_resid, 7 * h + c)
                    rhs = resid[:, :]
                if 7 * h + c > 0:
                    pe.wait_ge(s_oq, 7 * h + c)
                pe.matmul(ps[:, 3, P:2 * P], xT[:, c, :], rhs, start=True, stop=True).then_inc(s_y, 1)

            def update(h, c):
                pe.wait_ge(s_vnew, NT * h + c + 1)
                if c == 0 and h >= 1:
                    pe.wait_ge(s_o, NT * h)
                if c < NT - 1:
                    pe.matmul(ps[:, 4, 0:P], k_dec[h % 2][:, c, :], v_new[:, :], start=True, stop=True)\
                      .then_inc(s_su, 1)
                pe.matmul(ps[:, 2, P:2 * P], aT[h % 2][:, c, :], v_new[:, :], start=True, stop=True)\
                  .then_inc(s_av, 1)

            def transpose_out(h):
                pe.wait_ge(s_oscaled, h + 1)
                pe.wait_ge(s_m, NT * min(h + 2, GH))
                for b in range(2):
                    for c in range(4):
                        mm = pe.transpose(ps[:, 5 + b, c * P:(c + 1) * P], o_tok[:, 4 * b + c, :], ident[:, :])
                    mm.then_inc(s_ot, 1)

            for p, events in enumerate(PLANS):
                for kind, a, b in events:
                    if kind == "mm":
                        project(a, b)
                    elif kind == "T":
                        token_major(p - 1, a)
                    elif kind == "OT":
                        transpose_out(p - 3)
                    elif kind == "M" and a < NT:
                        scores(p - 1, a)
                    elif kind == "L":
                        level(b, a)
                    elif kind == "A":
                        with_state(b, a)
                    elif kind == "B":
                        solve(b, a)
                    elif kind == "C":
                        update(b, a)

            def out_stage(i):
                s = L[i]

                def turn(t):
                    pe.wait_ge(s["ln"], t + 1)
                    for b in range(2):
                        n = 2 * t + b
                        if n >= 4:
                            pe.wait_ge(s["xlo"], n - 3)
                        for k in range(4):
                            mm = pe.transpose(ps[:, 4 + n % 4, k * P:(k + 1) * P],
                                              tok[:, t, (4 * b + k) * P:(4 * b + k + 1) * P], ident[:, :])
                        mm.then_inc(s["xtr"], 1)

                for t in range(NT):
                    if t >= 2:
                        pe.wait_ge(s["yev"], 2 * (t - 1))
                    cut = slice(t * P, (t + 1) * P)
                    for k in range(NK):
                        if t == 0:
                            pe.wait_ge(s["olo"], k + 1)
                            pe.wait_ge(s["wolo"], k + 1)
                        for half in range(2):
                            for j in range(PASSES):
                                lhs = (act_hi, act_hi, act_lo)[j]
                                rhs = (wo_hi, wo_lo, wo_hi)[j]
                                mm = pe.matmul(ps[:, 2 * (t % 2) + half, :], lhs[:, k, cut],
                                               rhs[:, k, HALF * half:HALF * (half + 1)],
                                               start=(k == 0 and j == 0), stop=(k == NK - 1 and j == PASSES - 1))
                    mm.then_inc(s["y"], 1)
                    if i == 0 and t >= 1:
                        turn(t - 1)
                if i == 0:
                    turn(NT - 1)

            out_stage(0)
            if stop == 0:
                return

            pe.wait_ge(L[0]["xlo"], 2 * NT)

            def project_tokens(n):
                bl, t = n // NT, n % NT
                w = (256, HALF, HALF)[bl]
                if n >= 2:
                    pe.wait_ge(q_rope, n - 1)
                for k in range(NK):
                    sl = bl * NK + k
                    if t == 0:
                        pe.wait_ge(q_lo, sl + 1)
                    for j in range(PASSES):
                        lhs = (act_hi, act_hi, act_lo)[j]
                        rhs = (ws_hi, ws_lo, ws_hi)[j]
                        mm = pe.matmul(ps[:, n % 2, 0:w], lhs[:, k, t * P:(t + 1) * P], rhs[:, sl % WR, 0:w],
                                       start=(k == 0 and j == 0), stop=(k == NK - 1 and j == PASSES - 1))
                mm.then_inc(q_group, 1)

            def turn_tokens(n):
                pe.wait_ge(q_rope, n + 1)
                if n >= 2:
                    pe.wait_ge(q_tev, n - 1)
                for c in range(2 if n < NT else 4):
                    mm = pe.transpose(ps[:, 2 + n % 2, c * P:(c + 1) * P], qr[:, n % 2, c * P:(c + 1) * P], ident[:, :])
                mm.then_inc(q_tr, 1)

            for n in range(3 * NT):
                project_tokens(n)
                if n >= 1:
                    turn_tokens(n - 1)
            turn_tokens(3 * NT - 1)
            pe.wait_ge(q_tev, 3 * NT)
            pe.wait_ge(q_c, 6)

            def logits(u):
                jj, n = u // NT, u % NT
                if u >= 1:
                    pe.wait_ge(s_logit, u)
                for i in range(4):
                    r = 64 * (i % 2)
                    mm = pe.matmul(ps[:, 2 + i % 2, 256 * (i // 2):256 * (i // 2 + 1)],
                                   bT[r:r + 64, 2 * jj + i // 2, n * P:(n + 1) * P],
                                   kd[r:r + 64, jj // 2, n * P:(n + 2) * P], start=True, stop=True)
                mm.then_inc(s_s, 1)

            def project_gate(u):
                g = u // 2
                j, b = g // 2, g % 2
                if u % 2 == 0:
                    pe.wait_ge(z_los, j + 1)
                    if g >= 2:
                        pe.wait_ge(z_t, g - 1)
                for i in range(12 * (u % 2), 12 * (u % 2) + 12):
                    k, q = i // PASSES, i % PASSES
                    lhs = (z_hi, z_hi, z_lo)[q][j % 2]
                    rhs = (act_hi, act_lo, act_hi)[q]
                    mm = pe.matmul(ps[:, g % 2, :], lhs[:, k, :], rhs[:, k, HALF * b:HALF * (b + 1)],
                                   start=(i == 0), stop=(i == GROUP - 1))
                if u % 2:
                    mm.then_inc(z_group, 1)

            def turn_probs(u):
                pe.wait_ge(s_norm, u + 1)
                for w, done in ((0, s_pe0), (1, s_pe1)):
                    if u >= 1:
                        pe.wait_ge(done, u)
                    for i in range(4):
                        mm = pe.transpose(ps[:, 4 + w, i * P:(i + 1) * P], logit[:, u % 2, i, w * P:(w + 1) * P],
                                          ident[:, :])
                    mm.then_inc(s_pt, 1)

            def values(u):
                jj, n = u // NT, u % NT
                kv = jj // 2
                pe.wait_ge(s_pe0, u + 1)
                pe.wait_ge(s_pe1, u + 1)
                if u >= 2:
                    pe.wait_ge(s_ob, u - 1)
                for e in range(2):
                    for w in range(2):
                        mm = pe.matmul(ps[64 * e:64 * e + 64, 6 + u % 2, 0:256].rearrange("p (a q) -> p a q", a=2),
                                       vv[:, n + w, 64 * kv:64 * kv + 64],
                                       prob[:, u % 2, w, e::2, :], start=(w == 0), stop=(w == 1))
                mm.then_inc(s_pv, 1)

            for u in range(UNITS + 2):
                if u < UNITS:
                    logits(u)
                    project_gate(u)
                if 1 <= u <= UNITS:
                    turn_probs(u - 1)
                if u >= 2:
                    values(u - 2)
            out_stage(1)

        @block.scalar
        def _(act):
            own = Link(act, s_act)

            def fetch(w):
                if w >= 0:
                    act.wait_ge(s_wlo, w + 1)
                if w < 0:
                    act.dma_start(w_raw[:, :, 0:16], wa_tiles[:, :, GATE_COL:GDN_IN]).then_inc(s_wraw, 16)
                else:
                    c0 = P * channel_tile(w)
                    act.dma_start(w_raw[:, :, :], wa_tiles[:, :, c0:c0 + P]).then_inc(s_wraw, 16)

            def high(w):
                act.wait_ge(s_wraw, 16 * (w + 2))
                if w >= 1:
                    act.wait_ge(s_group, 2 * w)
                act.activation(w_hi[w % 2][:, :, :], w_raw[:, :, :], ACT.Copy).then_inc(s_whi, 1)

            fetch(-1)
            act.wait_ge(s_const, 5)
            high(-1)
            for n in range(2 * NT):
                act.wait_ge(s_xtr, n + 1)
                t, b = n // 2, n % 2
                act.activation(act_hi[:, 4 * b:4 * b + 4, t * P:(t + 1) * P],
                               ps[:, 4 + n % 4, :].rearrange("p (k q) -> p k q", k=4), ACT.Copy).then_inc(s_xhi, 1)
                if n == 1:
                    fetch(0)
            high(0)
            fetch(1)
            for b in range(2):
                act.wait_ge(s_group, b + 1)
                act.activation(gates[:, HALF * b:HALF * (b + 1)], ps[0:16, b, :], ACT.Copy).then_inc(s_gev, 1)
            act.wait_ge(s_gd, 1)
            act.activation(gt[:, 4], gt[:, 0], ACT.Exp).then_inc(s_ga, 1)
            act.wait_ge(s_gd, 2)
            own.next(act.activation(gt[:, 5], gt[:, 3], ACT.Exp))
            own.wait()
            act.activation(gt[:, 6], gt[:, 5], ACT.Ln, bias=1.0).then_inc(s_ga, 1)
            act.activation(bias2[:, 1, :], bias2[:, 1, :], ACT.Exp).then_inc(s_ga, 1)
            act.wait_ge(s_gd, 6)
            act.activation(sc["exp"][:, :, :], sc["gc"][:, :, :], ACT.Exp).then_inc(s_ga, 1)
            act.activation(sc["kdec"][:, :, :], gt[:, 1], ACT.Exp).then_inc(s_ga, 1)
            act.activation(sc["elast"][:, :, :], gt[:, 0], ACT.Exp).then_inc(s_ga, 1)

            def evacuate(g):
                b = g % 2
                act.wait_ge(s_group, g + 3)
                if g >= QKV_GROUPS:
                    if g == QKV_GROUPS:
                        act.wait_ge(s_silu, QKV_GROUPS)
                    else:
                        act.wait_ge(s_zt, g - QKV_GROUPS)
                    act.activation(th[:, :], ps[:, b, :], ACT.Tanh, scale=0.5).then_inc(s_zth, 1)
                    return
                if g >= 2:
                    act.wait_ge(s_tap, g - 1)
                    act.wait_ge(s_halo, g // 2)
                if b:
                    act.wait_ge(s_evac, g)
                    act.activation(xs[:, 1, 0:CONV_K - 1], xs[:, 0, HALF:HALF + CONV_K - 1], ACT.Copy)\
                       .then_inc(s_halo, 1)
                act.activation(xs[:, b, CONV_K - 1:], ps[:, b, :], ACT.Copy).then_inc(s_evac, 1)

            def gate_tanh(g):
                act.wait_ge(s_tap, g + 1)
                if g:
                    act.wait_ge(s_silu, g)
                act.activation(th[:, :], conv[:, :], ACT.Tanh).then_inc(s_th, 1)

            def token_major(h, i):
                act.wait_ge(s_tr, 2 * h + i + 1)
                if h >= 2:
                    act.wait_ge(s_av, NT * (h - 1))
                for q in range(4):
                    c = 4 * i + q
                    if NT * h + c:
                        act.wait_ge(s_sq, NT * h + c)
                    act.activation(sq_junk[:, 0, :], ps[:, 6, q * P:(q + 1) * P], ACT.Square,
                                   accum_out=sc["ssq"][:, h, c:c + 1]).then_inc(s_sq, 1)
                act.activation(v_tok[h % 2][:, 4 * i:4 * i + 4, :],
                               ps[:, 5, :].rearrange("p (c q) -> p c q", c=4), ACT.Copy).then_inc(s_tev, 1)
                act.wait_ge(s_kd, 2 * h + i + 1)
                for q in range(4):
                    c = 4 * i + q
                    if NT * h + c:
                        act.wait_ge(s_sk, NT * h + c)
                    act.activation(sq_junk[:, 1, :], ps[:, 7, q * P:(q + 1) * P], ACT.Square,
                                         accum_out=sc["ssk"][:, h, c:c + 1]).then_inc(s_sk, 1)

            def squares(h, c):
                act.wait_ge(s_o, NT * h + c + 1)
                if NT * h + c >= 2:
                    act.wait_ge(s_sso, NT * h + c - 1)
                act.activation(sso_junk[:, c % 2, :], o_tok[:, c, :], ACT.Square, accum_out=sc["sso"][:, h, c:c + 1])\
                   .then_inc(s_sso, 1)

            for p, events in enumerate(PLANS):
                h, o = p - 1, p - 3
                for kind, a, b in events:
                    r = b
                    if kind == "end":
                        evacuate(a)
                    elif kind == "piece" and a < QKV_GROUPS and b == 3:
                        gate_tanh(a)
                    elif kind == "weights":
                        high(a)
                    elif kind == "fetch":
                        fetch(a)
                    elif kind == "T":
                        token_major(h, a)
                    elif kind == "OF":
                        if o >= 0:
                            act.wait_ge(s_of, o + 1)
                            act.activation(sc["sso"][:, o, :], sc["sso"][:, o, :], ACT.Sqrt).then_inc(s_fs, 1)
                        if o + 1 < GH:
                            act.wait_ge(s_ak, o + 2)
                            act.activation(sc["rk"][:, o + 1, :], sc["rk"][:, o + 1, :], ACT.Sqrt).then_inc(s_rk, 1)
                    elif kind == "OT":
                        for q in range(2):
                            act.wait_ge(s_ot, 2 * o + q + 1)
                            act.activation(tok[:, o, HALF * q:HALF * (q + 1)], ps[:, 5 + q, :], ACT.Copy)\
                               .then_inc(s_otev, 1)
                    elif kind == "M":
                        if a < NT:
                            act.wait_ge(s_dp, NT * h + a + 1)
                            act.activation(decay[a % 2][:, :], decay[a % 2][:, :], ACT.Exp).then_inc(s_dt, 1)
                    elif kind == "L" and a == 0:
                        act.wait_ge(s_lv, 4 * r + 1)
                        src = ps[:, 6, 0:256].rearrange("p (c j) -> p c j", c=NT)
                        act.activation(uT[32:64, :, 0:32], src[32:64], ACT.Copy)
                        act.activation(uT[96:128, :, 0:32], src[96:128], ACT.Copy).then_inc(s_ut, 1)
                    elif kind == "L" and a == 2:
                        act.wait_ge(s_lv, 4 * r + 3)
                        act.activation(uT[64:128, :, :], ps[64:128, 6, :].rearrange("p (c j) -> p c j", c=NT),
                                       ACT.Copy).then_inc(s_ut, 1)
                    elif kind == "A" and a >= 1:
                        act.wait_ge(s_qs, 7 * r + a)
                        act.activation(q_state[:, :], ps[:, 3, 0:P], ACT.Copy, scale=sc["exp"][:, r, a:a + 1])\
                           .then_inc(s_oq, 1)
                        squares(r, a - 1)
                    elif kind == "B":
                        act.wait_ge(s_y, NT * r + a + 1)
                        act.activation(v_new[:, :], ps[:, 3, P:2 * P], ACT.Copy, scale=sc["cj"][:, r, a:a + 1])\
                           .then_inc(s_vnew, 1)
                    elif kind == "C" and a == NT - 1:
                        squares(r, a)

            def out_stage(i):
                s = L[i]
                src = (tok, bT)[i]
                if i == 0:
                    act.wait_ge(s_group, 2 * TILES + 2)
                else:
                    act.wait_ge(z_group, 2 * NK)
                for k in range(NK):
                    if i == 0:
                        act.wait_ge(s_gated, 2 * (k + 1))
                    else:
                        act.wait_ge(s_bg, k + 1)
                    act.activation(act_hi[:, k, :], src[:, k, :], ACT.Copy).then_inc(s["ohi"], 1)
                    if k == 0:
                        act.wait_ge((s_gated, s_bg)[i], (2 * GH, NK)[i])
                    act.wait_ge(s["wr"][k % 2], 16 * (k // 2 + 1))
                    act.activation(wo_hi[:, k, :], wo_raw[:, k % 2, :], ACT.Copy).then_inc(s["wohi"], 1)

                def high_x(t):
                    for b in range(2):
                        n = 2 * t + b
                        act.wait_ge(s["xtr"], n + 1)
                        act.activation(act_hi[:, 4 * b:4 * b + 4, t * P:(t + 1) * P],
                                       ps[:, 4 + n % 4, :].rearrange("p (k q) -> p k q", k=4), ACT.Copy)\
                           .then_inc(s["xhi"], 1)

                for t in range(NT):
                    act.wait_ge(s["st"], t + 1)
                    act.activation(mv[:, t % 2, 3:4], mv[:, t % 2, 2:3], ACT.Sqrt).then_inc(s["sqrt"], 1)
                    if i == 0 and t >= 1:
                        high_x(t - 1)
                if i == 0:
                    high_x(NT - 1)

            out_stage(0)
            if stop == 0:
                return
            act.wait_ge(L[0]["xlo"], 2 * NT)

            def high_slice(n):
                w = 256 if n < NK else HALF
                act.wait_ge(q_raw[n % 2], 16 * (n // 2 + 1))
                if n >= WR:
                    act.wait_ge(q_group, NT * ((n - WR) // NK + 1))
                act.activation(ws_hi[:, n % WR, 0:w], ws_raw[:, n % 2, 0:w], ACT.Copy).then_inc(q_hi, 1)

            for n in range(WR):
                high_slice(n)
            for n in range(3 * NT):
                bl, t = n // NT, n % NT
                if t == NT - 1:
                    for m in range(WR + bl * NK, min(WR + (bl + 1) * NK, SLICES)):
                        high_slice(m)
                act.wait_ge(q_tr, n + 1)
                if bl == 0:
                    act.activation(kd[:, :, (t + 1) * P:(t + 2) * P],
                                   ps[:, 2 + n % 2, 0:256].rearrange("p (a q) -> p a q", a=2), ACT.Copy)\
                       .then_inc(q_tev, 1)
                else:
                    act.activation(bT[:, 4 * (bl - 1):4 * bl, t * P:(t + 1) * P],
                                   ps[:, 2 + n % 2, :].rearrange("p (a q) -> p a q", a=4), ACT.Copy)\
                       .then_inc(q_tev, 1)

            def high_gate(j):
                act.wait_ge(z_rawd, 16 * (j + 1))
                if j >= 2:
                    act.wait_ge(z_group, 2 * (j - 1))
                act.activation(z_hi[j % 2][:, :, :], z_raw[:, :, :], ACT.Copy).then_inc(z_his, 1)

            high_gate(0)
            for u in range(UNITS + 2):
                if u < UNITS:
                    act.wait_ge(s_neg, u + 1)
                    for i in range(4):
                        act.activation(logit[:, u % 2, i, :], logit[:, u % 2, i, :], ACT.Exp,
                                       bias=sm["neg"][:, u % 2, i:i + 1], accum_out=sm["sum"][:, u % 2, i:i + 1])
                    act.activation(sm["sink"][:, u % 2, :], sm["off"][:, u % 2, :], ACT.Exp).then_inc(s_e, 1)
                if 1 <= u <= UNITS:
                    v = u - 1
                    act.wait_ge(s_pt, 2 * v + 1)
                    if v >= 2:
                        act.wait_ge(s_pv, v - 1)
                    act.activation(prob[:, v % 2, 0], ps[:, 4, :].rearrange("p (i q) -> p i q", i=4), ACT.Copy)\
                       .then_inc(s_pe0, 1)
                if u < UNITS and u % 2:
                    g = u // 2
                    act.wait_ge(z_group, g + 1)
                    if g:
                        act.wait_ge(z_t, g)
                    act.activation(zt[:, :], ps[:, g % 2, :], ACT.Tanh, scale=0.5).then_inc(z_th, 1)
                if u % 4 == 1 and u // 4 + 1 < NK:
                    high_gate(u // 4 + 1)
            out_stage(1)

        @block.vector
        def _(dve):
            own = Link(dve, s_dve)

            def low(w):
                dve.wait_ge(s_whi, w + 2)
                dve.tensor_tensor(w_lo[w % 2][:, :, :], w_raw[:, :, :], w_hi[w % 2][:, :, :].bitcast(F32),
                                  ALU.subtract).then_inc(s_wlo, 1)

            low(-1)
            for n in range(2 * NT):
                dve.wait_ge(s_xhi, n + 1)
                t, b = n // 2, n % 2
                cut = (slice(None), slice(4 * b, 4 * b + 4), slice(t * P, (t + 1) * P))
                dve.tensor_tensor(act_lo[cut], ps[:, 4 + n % 4, :].rearrange("p (k q) -> p k q", k=4),
                                  act_hi[cut].bitcast(F32), ALU.subtract).then_inc(s_xlo, 1)
            low(0)
            dve.wait_ge(s_ctr, 1)
            dve.tensor_scalar(convw[:, :, :], ps[:, 2, 0:CONV_K * QKV_TILES].rearrange("p (w k) -> p k w", k=CONV_K),
                              0.5, None, ALU.mult).then_inc(s_cw, 1)
            own.next(dve.tensor_scalar(norm_g[:, :], norm_g[:, :], 0.5, None, ALU.mult))
            dve.wait_ge(s_gtr, 1)
            lg = ps[:, 3, 0:P].rearrange("p (c j) -> p j c", c=NT)
            own.next(dve.tensor_tensor(gt[:, 1], lg[:, GH:2 * GH, :],
                                       bias2[:, 0, :].unsqueeze(2).broadcast_to([P, GH, NT]), ALU.add))
            dve.tensor_scalar(gt[:, 0], lg[:, 0:GH, :], -1.0, 80.0, ALU.mult, ALU.min).then_inc(s_gd, 1)
            own.wait()
            own.next(dve.tensor_scalar(gt[:, 2], gt[:, 1], -1.0, None, ALU.mult))
            own.wait()
            dve.tensor_tensor(gt[:, 3], gt[:, 1], gt[:, 2], ALU.min).then_inc(s_gd, 1)
            dve.wait_ge(s_ga, 3)
            own.next(dve.scalar_tensor_tensor(gt[:, 2], gt[:, 1], 0.0, gt[:, 6], ALU.max, ALU.add))
            own.next(dve.tensor_scalar(gt[:, 7], gt[:, 4], 1.0, None, ALU.add))
            own.wait()
            dve.scalar_tensor_tensor(sc["g"][:, :, :], gt[:, 2], -1.0,
                                     bias2[:, 1, :].unsqueeze(2).broadcast_to([P, GH, NT]), ALU.mult, ALU.mult)\
               .then_inc(s_gd, 1)
            own.next(dve.reciprocal(sc["beta"][:, :, :], gt[:, 7]))
            dve.wait_ge(s_gc, 1)
            gcp = ps[:, 3, 128:192].rearrange("p (h c) -> p h c", h=GH)
            glp = ps[:, 3, 192:256].rearrange("p (h c) -> p h c", h=GH)
            dve.tensor_copy(sc["gc"][:, :, :], gcp).then_inc(s_gd, 1)
            dve.tensor_copy(gt[:, 0], glp).then_inc(s_gd, 1)
            dve.wait_ge(s_gd, 5)
            dve.tensor_tensor(gt[:, 1], gt[:, 0], sc["gc"][:, :, :], ALU.subtract).then_inc(s_gd, 1)
            dve.wait_ge(s_ga, 6)
            own.next(dve.tensor_scalar(sc["nexp"][:, :, :], sc["exp"][:, :, :], -1.0, None, ALU.mult))
            dve.wait_ge(s_cw, 1)

            def piece(g, k):
                w, b = g // 2, g % 2
                if g >= QKV_GROUPS:
                    zacc = xs[:, b, CONV_K - 1:]
                    z = g - QKV_GROUPS
                    if k == 0:
                        dve.wait_ge(s_zth, z + 1)
                        dve.wait_ge(s_tap, QKV_GROUPS)
                        if z >= 2:
                            dve.wait_ge(s_gated, z - 1)
                        dve.scalar_tensor_tensor(zacc, th[:, :], 1.0, ps[:, b, :], ALU.add, ALU.mult).then_inc(s_zt, 1)
                    else:
                        dve.wait_ge(s_zt, z + 1)
                        dve.wait_ge(s_otev, 2 * (z // 2) + 2)
                        dst = tok[:, z // 2, HALF * b:HALF * (b + 1)]
                        dve.scalar_tensor_tensor(dst, zacc, norm_g[:, 0:1], dst, ALU.mult, ALU.mult)\
                           .then_inc(s_gated, 1)
                    return
                h = g // 6
                tile = channel_tile(w)
                if k == 0:
                    dve.wait_ge(s_evac, g + 1)
                    if g:
                        dve.wait_ge(s_silu, g)
                    if b:
                        dve.wait_ge(s_halo, g // 2 + 1)
                    own.next(dve.tensor_scalar(conv[:, :], xs[:, b, 0:HALF], convw[:, 0, tile:tile + 1], None, ALU.mult))
                elif k < CONV_K:
                    own.wait()
                    ins = dve.scalar_tensor_tensor(conv[:, :], xs[:, b, k:k + HALF], convw[:, k, tile:tile + 1], conv[:, :],
                                                   ALU.mult, ALU.add)
                    if k == CONV_K - 1:
                        ins.then_inc(s_tap, 1)
                    else:
                        own.next(ins)
                else:
                    dve.wait_ge(s_th, g + 1)
                    kind = w % 3
                    if kind == 2:
                        if h >= 1:
                            dve.wait_ge(s_tr, 2 * h)
                        dst = vT
                    else:
                        if h >= 3:
                            dve.wait_ge(s_y, NT * (h - 2))
                        dst = (qT, kT)[kind][h % 3]
                    dve.scalar_tensor_tensor(dst[:, HALF * b:HALF * (b + 1)], th[:, :], 1.0, conv[:, :],
                                             ALU.add, ALU.mult).then_inc(s_silu, 1)

            def scalars(h):
                dve.wait_ge(s_sk, NT * (h + 1))
                dve.tensor_scalar(sc["rk"][:, h, :], sc["ssk"][:, h, :], EPS, None, ALU.add).then_inc(s_ak, 1)
                dve.wait_ge(s_ak, h + 1)
                own.next(dve.tensor_scalar(sc["ssk"][:, h, :], sc["ssk"][:, h, :], EPS, None, ALU.add))
                own.wait()
                own.next(dve.reciprocal(sc["ssk"][:, h, :], sc["ssk"][:, h, :]))
                own.next(dve.tensor_scalar(sc["aq"][:, h, :], sc["ssq"][:, h, :], EPS, P * EPS, ALU.add, ALU.mult))
                own.wait()
                own.next(dve.tensor_tensor(sc["cj"][:, h, :], sc["ssk"][:, h, :], sc["beta"][:, h, :], ALU.mult))
                own.wait()
                own.next(dve.tensor_scalar(sc["ncj"][:, h, :], sc["cj"][:, h, :], -1.0, None, ALU.mult))

            def exponents(h, c):
                dve.wait_ge(s_gcr, NT * h + c + 1)
                if NT * h + c >= 2:
                    dve.wait_ge(s_m, NT * h + c - 1)
                dve.scalar_tensor_tensor(decay[c % 2][:, :], ps[:, 7, 0:P], sc["gc"][:, h, c:c + 1], causal[:, :],
                                         ALU.subtract, ALU.min).then_inc(s_dp, 1)

            def matrices(h, c):
                dve.wait_ge(s_dt, NT * h + c + 1)
                dve.wait_ge(s_kk, NT * h + c + 1)
                bank = 5 + c % 2
                if c == 0:
                    own.wait()
                own.next(dve.scalar_tensor_tensor(nT[h % 2][:, c, :], ps[:, bank, 0:P], sc["ncj"][:, h, c:c + 1],
                                                  decay[c % 2][:, :], ALU.mult, ALU.mult))
                dve.tensor_tensor(aT[h % 2][:, c, :], ps[:, bank, P:2 * P], decay[c % 2][:, :], ALU.mult)\
                   .then_inc(s_m, 1)

            for p, events in enumerate(PLANS):
                h, o = p - 1, p - 3
                for kind, a, b in events:
                    r = b
                    if kind == "piece":
                        piece(a, b)
                    elif kind == "low":
                        low(a)
                    elif kind == "OF":
                        if o >= 0:
                            dve.wait_ge(s_sso, NT * (o + 1))
                            dve.scalar_tensor_tensor(sc["sso"][:, o, :], sc["sso"][:, o, :], 1.0 / P,
                                                     sc["aq"][:, o, :], ALU.mult, ALU.add).then_inc(s_of, 1)
                    elif kind == "T":
                        dve.wait_ge(s_tr, 2 * h + a + 1)
                        if h >= 2:
                            dve.wait_ge(s_av, NT * (h - 1))
                        dve.tensor_tensor(k_dec[h % 2][:, 4 * a:4 * a + 4, :],
                                          ps[:, 7, :].rearrange("p (c q) -> p c q", c=4),
                                          sc["kdec"][:, h, 4 * a:4 * a + 4].unsqueeze(2).broadcast_to([P, 4, P]),
                                          ALU.mult).then_inc(s_kd, 1)
                    elif kind == "VS":
                        v = p - 2
                        dve.wait_ge(s_rk, v + 1)
                        dve.tensor_tensor(v_tok[v % 2][:, :, :], v_tok[v % 2][:, :, :],
                                          sc["rk"][:, v, :].unsqueeze(2).broadcast_to([P, NT, P]), ALU.mult)\
                           .then_inc(s_vs, 1)
                    elif kind == "OS":
                        dve.wait_ge(s_fs, o + 1)
                        own.next(dve.reciprocal(sc["aq"][:, o, :], sc["sso"][:, o, :]))
                        own.wait()
                        dve.tensor_tensor(o_tok[:, :, :], o_tok[:, :, :],
                                          sc["aq"][:, o, :].unsqueeze(2).broadcast_to([P, NT, P]), ALU.mult)\
                           .then_inc(s_oscaled, 1)
                    elif kind == "M":
                        if a == 0:
                            scalars(h)
                        if a < NT:
                            exponents(h, a)
                        if a >= 1:
                            matrices(h, a - 1)
                    elif kind == "X":
                        dve.wait_ge(s_xt, 64 * (r + 1))
                        if r >= 1:
                            dve.wait_ge(s_ot, 2 * r)
                        dve.memset(xr[0:32, :, 32:64], 0.0)
                        dve.transpose(xr[0:32, :, 0:32], xT[0:32, :, 0:32])
                        dve.transpose(xr[32:64, :, 32:64], xT[32:64, :, 32:64])
                        dve.transpose(xr[64:96, :, 0:32], xT[64:96, :, 64:96]).then_inc(s_xr, 1)
                    elif kind == "L" and a == 1:
                        dve.wait_ge(s_lv, 4 * r + 2)
                        src = ps[:, 7, 0:256].rearrange("p (c j) -> p c j", c=NT)
                        dve.tensor_copy(xT[0:32, :, 32:64], src[0:32])
                        dve.tensor_copy(xT[64:96, :, 96:128], src[64:96])
                        dve.tensor_copy(xr[32:64, :, 0:32], src[32:64]).then_inc(s_xl, 1)
                    elif kind == "L" and a == 3:
                        dve.wait_ge(s_lv, 4 * r + 4)
                        dve.tensor_copy(xT[0:64, :, 64:128], ps[0:64, 7, :].rearrange("p (c j) -> p c j", c=NT))\
                           .then_inc(s_xl, 1)
                    elif kind == "A" and a >= 1:
                        dve.wait_ge(s_ks, 7 * r + a)
                        if a == 1:
                            dve.wait_ge(s_vs, r + 1)
                        dve.scalar_tensor_tensor(resid[:, :], ps[:, 2, 0:P], sc["nexp"][:, r, a:a + 1],
                                                 v_tok[r % 2][:, a, :], ALU.mult, ALU.add).then_inc(s_resid, 1)
                    elif kind == "C":
                        if a < NT - 1:
                            dve.wait_ge(s_su, 7 * r + a + 1)
                            if a == 0:
                                dve.tensor_copy(state[:, :], ps[:, 4, 0:P]).then_inc(s_state, 1)
                            else:
                                dve.wait_ge(s_state, 7 * r + a)
                                dve.scalar_tensor_tensor(state[:, :], state[:, :], sc["elast"][:, r, a:a + 1],
                                                         ps[:, 4, 0:P], ALU.mult, ALU.add).then_inc(s_state, 1)
                        dve.wait_ge(s_av, NT * r + a + 1)
                        if a == 0:
                            dve.tensor_copy(o_tok[:, 0, :], ps[:, 2, P:2 * P]).then_inc(s_o, 1)
                        else:
                            dve.wait_ge(s_oq, 7 * r + a)
                            dve.tensor_tensor(o_tok[:, a, :], ps[:, 2, P:2 * P], q_state[:, :], ALU.add)\
                               .then_inc(s_o, 1)

            def out_stage(i):
                s = L[i]
                src = (tok, bT)[i]
                own = Link(dve, s["dve"])
                for k in range(NK):
                    dve.wait_ge(s["ohi"], k + 1)
                    dve.tensor_tensor(act_lo[:, k, :], src[:, k, :], act_hi[:, k, :].bitcast(F32), ALU.subtract)\
                       .then_inc(s["olo"], 1)
                    dve.wait_ge(s["wohi"], k + 1)
                    dve.tensor_tensor(wo_lo[:, k, :], wo_raw[:, k % 2, :], wo_hi[:, k, :].bitcast(F32),
                                      ALU.subtract).then_inc(s["wolo"], 1)

                def low_x(t):
                    for b in range(2):
                        n = 2 * t + b
                        dve.wait_ge(s["xhi"], n + 1)
                        cut = (slice(None), slice(4 * b, 4 * b + 4), slice(t * P, (t + 1) * P))
                        dve.tensor_tensor(act_lo[cut], ps[:, 4 + n % 4, :].rearrange("p (k q) -> p k q", k=4),
                                          act_hi[cut].bitcast(F32), ALU.subtract).then_inc(s["xlo"], 1)

                dve.wait_ge(s["params"], 32)
                for t in range(NT):
                    q = t % 2
                    dve.wait_ge(s["y"], t + 1)
                    if i == 0:
                        dve.wait_ge(s["x"][q], 16 * (t // 2 + 1))
                    elif t >= 2:
                        dve.wait_ge(s["o"][q], 16 * (t // 2))
                    if t:
                        dve.wait_ge(s["ln"], t)
                    x_old = xres[:, q, :] if i == 0 else tok[:, t, :]
                    for half in range(2):
                        cut = slice(HALF * half, HALF * (half + 1))
                        dve.scalar_tensor_tensor(yr[:, q, cut], x_old[:, cut], ALPHA, ps[:, 2 * q + half, :],
                                                 ALU.mult, ALU.add).then_inc(s["yev"], 1)
                    for half in range(2):
                        dve.wait_ge(s["yev"], 2 * t + half + 1)
                        own.next(dve.bn_stats(stats[:, q, half, :], yr[:, q, HALF * half:HALF * (half + 1)]))
                    own.wait()
                    own.next(dve.bn_aggr(mv[:, q, 0:2], stats[:, q, :, :].rearrange("p a b -> p (a b)")))
                    own.wait()
                    dve.tensor_scalar(mv[:, q, 2:3], mv[:, q, 1:2], LN_EPS, None, ALU.add).then_inc(s["st"], 1)
                    dve.wait_ge(s["sqrt"], t + 1)
                    own.next(dve.reciprocal(mv[:, q, 3:4], mv[:, q, 3:4]))
                    own.wait()
                    own.next(dve.tensor_scalar(yr[:, q, :], yr[:, q, :], mv[:, q, 0:1], mv[:, q, 3:4],
                                               ALU.subtract, ALU.mult))
                    own.wait()
                    own.next(dve.tensor_tensor(yr[:, q, :], yr[:, q, :], lng[:, :], ALU.mult))
                    own.wait()
                    dst = tok[:, t, :] if i == 0 else yr[:, q, :]
                    dve.tensor_tensor(dst, yr[:, q, :], lnb[:, :], ALU.add).then_inc(s["ln"], 1)
                    if i == 0 and t >= 1:
                        low_x(t - 1)
                if i == 0:
                    low_x(NT - 1)

            out_stage(0)
            if stop == 0:
                return
            own = Link(dve, q_dve)

            def low_slice(n):
                w = 256 if n < NK else HALF
                dve.wait_ge(q_hi, n + 1)
                dve.tensor_tensor(ws_lo[:, n % WR, 0:w], ws_raw[:, n % 2, 0:w], ws_hi[:, n % WR, 0:w].bitcast(F32),
                                  ALU.subtract).then_inc(q_lo, 1)

            for n in range(WR):
                low_slice(n)
            dve.wait_ge(q_small, 48)
            for n in range(3 * NT):
                bl, t = n // NT, n % NT
                if t == NT - 1:
                    for m in range(WR + bl * NK, min(WR + (bl + 1) * NK, SLICES)):
                        low_slice(m)
                dve.wait_ge(q_group, n + 1)
                if n >= 2:
                    dve.wait_ge(q_tr, n - 1)
                heads = KVH if bl == 0 else 8
                w = heads * HD
                src = ps[:, n % 2, 0:w].rearrange("p (h d) -> p h d", h=heads)
                a = rot[:, 0, 0:w].rearrange("p (h d) -> p h d", h=heads)
                b = rot[:, 1, 0:w].rearrange("p (h d) -> p h d", h=heads)
                cs = cosr[:, t:t + 1, :].broadcast_to([P, heads, HD])
                lo_sin = sinr[:, t:t + 1, 0:HD // 2].broadcast_to([P, heads, HD // 2])
                hi_sin = sinr[:, t:t + 1, HD // 2:HD].broadcast_to([P, heads, HD // 2])
                if n:
                    dve.wait_ge(q_rope, n)
                own.next(dve.tensor_tensor(a, src, cs, ALU.mult))
                own.next(dve.tensor_tensor(b[:, :, 0:HD // 2], src[:, :, HD // 2:HD], lo_sin, ALU.mult))
                own.next(dve.tensor_tensor(b[:, :, HD // 2:HD], src[:, :, 0:HD // 2], hi_sin, ALU.mult))
                if bl == 0:
                    own.next(dve.tensor_copy(vv[:, t + 1, :], ps[:, n % 2, P:2 * P]))
                own.wait()
                if bl == 0:
                    dst = qr[:, n % 2, 0:2 * w].rearrange("p (h e d) -> p h e d", h=KVH, e=2)
                    own.next(dve.tensor_tensor(dst[:, :, 0, :], a, b, ALU.add))
                    dve.tensor_tensor(dst[:, :, 1, :], a, b, ALU.add).then_inc(q_rope, 1)
                else:
                    dve.tensor_tensor(qr[:, n % 2, :].rearrange("p (h d) -> p h d", h=heads), a, b, ALU.add)\
                       .then_inc(q_rope, 1)

            def low_gate(j):
                dve.wait_ge(z_his, j + 1)
                dve.tensor_tensor(z_lo[j % 2][:, :, :], z_raw[:, :, :], z_hi[j % 2][:, :, :].bitcast(F32),
                                  ALU.subtract).then_inc(z_los, 1)

            low_gate(0)
            dve.wait_ge(q_c, 6)
            for u in range(UNITS + 2):
                if u < UNITS:
                    jj, n, q = u // NT, u % NT, u % 2
                    dve.wait_ge(s_s, u + 1)
                    if u >= 2:
                        dve.wait_ge(s_pt, 2 * (u - 1))
                        dve.wait_ge(s_neg, u - 1)
                    for i in range(4):
                        head = 4 * jj + i
                        ins = dve.tensor_tensor_reduce(logit[:, q, i, :],
                                                       ps[:, 2 + i % 2, 256 * (i // 2):256 * (i // 2 + 1)],
                                                       window[:, min(n, 1), :], SCALE, sinks[:, head:head + 1],
                                                       ALU.add, ALU.max, sm["max"][:, q, i:i + 1])
                        if i == 3:
                            ins.then_inc(s_logit, 1)
                        else:
                            own.next(ins)
                    own.wait()
                    dve.wait_ge(s_logit, u + 1)
                    own.next(dve.tensor_scalar(sm["neg"][:, q, :], sm["max"][:, q, :], -1.0, None, ALU.mult))
                    dve.tensor_tensor(sm["off"][:, q, :], sinks[:, 4 * jj:4 * jj + 4], sm["max"][:, q, :],
                                      ALU.subtract).then_inc(s_neg, 1)
                if 1 <= u <= UNITS:
                    v = u - 1
                    q = v % 2
                    dve.wait_ge(s_pt, 2 * v + 2)
                    if v >= 2:
                        dve.wait_ge(s_pv, v - 1)
                    dve.tensor_copy(prob[:, q, 1], ps[:, 5, :].rearrange("p (i q) -> p i q", i=4)).then_inc(s_pe1, 1)
                if u < UNITS:
                    q = u % 2
                    dve.wait_ge(s_e, u + 1)
                    if u >= 2:
                        dve.wait_ge(s_norm, u - 1)
                    own.next(dve.tensor_tensor(sm["den"][:, q, :], sm["sum"][:, q, :], sm["sink"][:, q, :], ALU.add))
                    own.wait()
                    own.next(dve.reciprocal(sm["rden"][:, q, :], sm["den"][:, q, :]))
                    own.wait()
                    for i in range(4):
                        ins = dve.tensor_scalar(logit[:, q, i, :], logit[:, q, i, :], sm["rden"][:, q, i:i + 1], None,
                                                ALU.mult)
                        if i == 3:
                            ins.then_inc(s_norm, 1)
                        else:
                            own.next(ins)
                if u >= 2:
                    v = u - 2
                    jj, n = v // NT, v % NT
                    dve.wait_ge(s_pv, v + 1)
                    dve.tensor_copy(bT[:, 2 * jj:2 * jj + 2, n * P:(n + 1) * P],
                                    ps[:, 6 + v % 2, 0:256].rearrange("p (a q) -> p a q", a=2)).then_inc(s_ob, 1)
                    if n == NT - 1:
                        dve.wait_ge(s_ob, v + 1)
                        dve.wait_ge(z_t, 4 * (jj + 1))
                        for i in range(2):
                            dve.scalar_tensor_tensor(bT[:, 2 * jj + i, :], zg[:, i, :], 0.5, bT[:, 2 * jj + i, :],
                                                     ALU.mult, ALU.mult).then_inc(s_bg, 1)
                if u < UNITS and u % 2:
                    g = u // 2
                    j, b = g // 2, g % 2
                    dve.wait_ge(z_th, g + 1)
                    if j >= 2:
                        dve.wait_ge(s_bg, 2 * (j // 2))
                    dve.scalar_tensor_tensor(zg[:, j % 2, HALF * b:HALF * (b + 1)], zt[:, :], 1.0, ps[:, g % 2, :],
                                             ALU.add, ALU.mult).then_inc(z_t, 1)
                if u % 4 == 1 and u // 4 + 1 < NK:
                    low_gate(u // 4 + 1)
            out_stage(1)


_INS = ["x", "a_w_in", "a_conv", "a_a_log", "a_dt_bias", "a_norm_g", "a_w_out", "b_w_in", "b_sinks", "b_w_out",
        "ln_g", "ln_b"]


def rope_tables():
    half = HD // 2
    inv = np.float32(10000.0) ** (-np.arange(half, dtype=np.float32) / np.float32(half))
    ang = np.arange(SEQ, dtype=np.float32)[:, None] * inv[None, :]
    cos, sin = np.cos(ang), np.sin(ang)
    return (np.concatenate([cos, cos], axis=1).astype(np.float32),
            np.concatenate([-sin, sin], axis=1).astype(np.float32))


def kernel(**inputs):
    import concourse.bacc as _bacc
    from concourse.bass_utils import run_bass_kernel_spmd as _run

    nc = _bacc.Bacc("TRN2", target_bir_lowering=False, num_devices=1)
    cos, sin = rope_tables()
    named = [(n, np.ascontiguousarray(inputs[n])) for n in _INS] + [("rope_cos", cos), ("rope_sin", sin)]
    arrays, args = {}, []
    for name, a in named:
        arrays[f"in_{name}"] = a
        args.append(nc.dram_tensor(f"in_{name}", a.shape, mybir.dt.from_np(a.dtype), kind="ExternalInput").ap())
    args.append(nc.dram_tensor("out_0", (1, SEQ, DM), F32, kind="ExternalOutput").ap())
    hybrid_trunk(nc, *args)
    r = _run(nc, [arrays], core_ids=[0])
    return r.results[0]["out_0"]
```

```python
from contextlib import ExitStack

import numpy as np

import concourse.bass as bass
from concourse import mybir

F32 = mybir.dt.float32
F32R = mybir.dt.float32r
ALU = mybir.AluOpType
ACT = mybir.ActivationFunctionType

P = 128
SEQ = 1024
DM = 1024
NT = SEQ // P
NK = DM // P
HALF = 512
ALPHA = float(4 ** 0.25)
EPS = 1e-6
LN_EPS = 1e-5
NEG = -1e30

GH = 8
CONV_K = 4
QKV_TILES = 3 * GH
TILES = QKV_TILES + GH
GDN_IN = 4112
GATE_COL = 128 * TILES
QKV_GROUPS = 2 * QKV_TILES

SH = 16
HD = 64
KVH = 2
SWA_Z0 = 1280
SCALE = HD ** -0.5
UNITS = SH // 4 * NT
WR = 9
SLICES = 2 * NK
TOKEN_BANKS = (0, 1, 6, 7)

PASSES = 3
GROUP = NK * PASSES
STEP = 3


AT_ROOTS, AT_SCALE, AT_OUT = 0.1277, 0.1535, 0.215
AT_VALUES = 0.2498
AT_TOKEN = (0.2269, 0.2663)
AT_MATRIX, AT_MATRIX_STEP = 0.2837, 0.0233
AT_BLOCKS, AT_INVERSE, AT_INVERSE_STEP = 0.4843, 0.504, 0.0197
AT_SCAN, AT_SCAN_STEP = 0.5696, 0.0238
LAST_BLOCKS, LAST_INVERSE, LAST_SCAN, LAST_SCAN_STEP = 0.2209, 0.3486, 0.4255, 0.0229


GATE_FROM = 18
GATE_SPLIT = 10
OUT_BANKS = (0, 2, 4, 0, 2, 0, 2, 0)
EARLY = (3, 1)


def slices_before(n, refill):
    if n < 2:
        return (2 * n, 2 * n + 1)
    if n < WR - 2:
        return (n + 2,)
    return range(WR, SLICES) if n == refill else ()


LAG_SCALAR = {"end": 1.7, "piece": 5.5, "A": 1.6, "B": 0.3, "M": 3.0, "T": 0.6, "L": 6.3}
LAG_VECTOR = {"piece": 0.9, "A": 0.1, "C": 0, "M": 0.8, "T": 1.9, "L": 7.5}


def plan(p, lag):
    if p < GH:
        groups = list(range(6 * p, 6 * p + 6))
    elif p == GH:
        groups = list(range(QKV_GROUPS, QKV_GROUPS + GATE_SPLIT))
    elif p == GH + 1:
        groups = list(range(QKV_GROUPS + GATE_SPLIT, 2 * TILES))
    else:
        groups = []
    last = 2 * TILES - 2
    events = []
    for i, g in enumerate(groups):
        t0 = GROUP * i
        for q in range(0, GROUP, STEP):
            events.append((t0 + q, 0, ("mm", g, q)))
        end = t0 + GROUP - 0.5
        events.append((end, 1, ("end", g, 0)))
        if g % 2 == 0 and g // 2 + 1 < TILES:
            events.append((t0 + 6.6, 1, ("weights", g // 2 + 1, 0)))
            if g // 2 + 2 < TILES:
                events.append((t0 + 15.9, 1, ("fetch", g // 2 + 2, 0)))
        if g % 2 == 0 and g // 2 + 1 < TILES:
            events.append((t0 + 6.8, 1, ("low", g // 2 + 1, 0)))
        for k in range(5 if g < QKV_GROUPS else 2):
            if g < last:
                events.append((end + 0.58 + k * 5.56, 2, ("piece", g, k)))
            elif k == 0:
                events.append((end + 0.2, 2, ("piece", g, k)))
    span = GROUP * max(len(groups), 1)
    slots = []
    if 0 <= p - 3 < GH or 0 <= p - 2 < GH:
        slots += [(AT_ROOTS, ("OF", 0))]
    if 0 <= p - 3 < GH:
        slots += [(AT_SCALE, ("OS", 0)), (AT_OUT, ("OT", 0))]
    if p == GH + 2:
        slots += [(0.1 + 0.2 * k, ("W", k)) for k in range(EARLY[0])]
    if 0 <= p - 2 < GH:
        slots += [(AT_VALUES, ("VS", 0))]
    if 0 <= p - 1 < GH:
        slots += [(AT_TOKEN[i], ("T", i)) for i in range(2)]
        slots += [(AT_MATRIX + AT_MATRIX_STEP * c, ("M", c)) for c in range(NT + 1)]
    for r in (p - 3, p - 2):
        if 0 <= r < GH:
            blocks, inverse, scan, step = (AT_BLOCKS, AT_INVERSE, AT_SCAN, AT_SCAN_STEP) if r < GH - 1 else \
                                          (LAST_BLOCKS, LAST_INVERSE, LAST_SCAN, LAST_SCAN_STEP)
            items = [(blocks, ("X", 0))] + [(inverse + AT_INVERSE_STEP * i, ("L", i)) for i in range(4)]
            items += [(scan + step * (3 * c + i), ("ABC"[i], c)) for c in range(NT) for i in range(3)]
            shift = p - 2 - r
            slots += [(at - shift, (n, c, r)) for at, (n, c) in items if 0 <= at - shift < 1]
    for at, item in slots:
        events.append((at * span, 3, (item + (0,))[:3]))
    events.sort(key=lambda e: (e[0] + lag.get(e[2][0], 0.0), e[1]))
    out = [e[2] for e in events]
    if p == GH + 2:
        out += [("piece", last, 1), ("piece", last + 1, 1)]
    return out


PLANS, SCALAR_PLANS, VECTOR_PLANS = ([plan(p, lag) for p in range(GH + 3)] for lag in ({}, LAG_SCALAR, LAG_VECTOR))


class Link:

    def __init__(self, eng, sem):
        self.eng, self.sem, self.n = eng, sem, 0

    def next(self, ins):
        ins.then_inc(self.sem, 1)
        self.n += 1

    def wait(self):
        self.eng.wait_ge(self.sem, self.n)


def hybrid_trunk(nc, x, a_w_in, a_conv, a_a_log, a_dt_bias, a_norm_g, a_w_out, b_w_in, b_sinks, b_w_out,
                 ln_g, ln_b, rope_cos, rope_sin, out):
    wa = a_w_in[0]
    wb = b_w_in[0]
    w_out = [a_w_out[0], b_w_out[0]]
    blocks_in = nc.dram_tensor("blocks_in", [2, NT * 4, 32, 32], F32).ap()
    gc_rows = nc.dram_tensor("gc_rows", [16, HALF], F32).ap()
    blocks_out = nc.dram_tensor("blocks_out", [2, NT * 4, 32, 32], F32).ap()
    ctx = ExitStack()
    with ctx:
        def sem(name):
            return ctx.enter_context(nc.semaphore(name))

        taken = [0]

        def sbuf(stack, name, shape, dt=F32):
            taken[0] += -(-4 * int(np.prod(shape[1:])) // 32) * 32
            return stack.enter_context(nc.sbuf_tensor(name, shape, dt))

        ps = ctx.enter_context(nc.psum_tensor("ps", [P, 8, HALF], F32))

        act_hi = sbuf(ctx, "act_hi", [P, NK, SEQ], F32R)
        act_lo = sbuf(ctx, "act_lo", [P, NK, SEQ], F32R)
        tok = sbuf(ctx, "tok", [P, NT, SEQ])
        ident = sbuf(ctx, "ident", [P, P])

        taken[0] = 0
        st = ExitStack()
        qT, kT, k_dec, v_tok, aT, nT = [None] * 3, [None] * 3, [None] * 2, [None] * 2, [None] * 2, [None] * 2

        def ring_buffers(slots, odd):
            for i in slots:
                qT[i] = sbuf(st, f"qT{i}", [P, SEQ])
                kT[i] = sbuf(st, f"kT{i}", [P, SEQ])
            nT[odd] = sbuf(st, f"nT{odd}", [P, NT, P])

        def chunk_buffers(odd):
            k_dec[odd] = sbuf(st, f"k_dec{odd}", [P, NT, P])
            v_tok[odd] = sbuf(st, f"v_tok{odd}", [P, NT, P])
            aT[odd] = sbuf(st, f"aT{odd}", [P, NT, P])

        ring_buffers((1,), 1)
        chunk_buffers(1)
        xT = sbuf(st, "xT", [P, NT, P])
        o_tok = sbuf(st, "o_tok", [P, NT, P])
        o_flat = o_tok[:, :, :].rearrange("p a b -> p (a b)")
        xr = o_flat[:, 0:NT * 64].rearrange("p (c j) -> p c j", c=NT)
        uT = o_flat[:, NT * 64:NT * 128].rearrange("p (c j) -> p c j", c=NT)
        ring_buffers((0, 2), 0)
        w_raw = sbuf(st, "w_raw", [P, NK, P])
        w_hi = [sbuf(st, f"w_hi{i}", [P, NK, P], F32R) for i in range(2)]
        w_lo = [sbuf(st, f"w_lo{i}", [P, NK, P], F32R) for i in range(2)]
        conv = sbuf(st, "conv", [P, HALF])
        state = sbuf(st, "state", [P, P])
        resid = sbuf(st, "resid", [P, P])
        q_state = sbuf(st, "q_state", [P, P])
        v_new = sbuf(st, "v_new", [P, P])
        decay = [sbuf(st, f"decay{i}", [P, P]) for i in range(2)]
        half = ExitStack()
        blocks = sbuf(half, "blocks", [32, 32, 32])
        half.close()
        taken[0] -= 4 * 1024
        gc_table = sbuf(st, "gc_table", [P, 1024], F32R)[64:128, 0:HALF]
        chosen = sbuf(st, "chosen", [P, 16], F32R)
        rank1 = sbuf(st, "rank1", [32, 256])
        tri = sbuf(st, "tri", [P, P])
        causal = sbuf(st, "causal", [P, P])
        bias2 = sbuf(st, "bias2", [P, 2, GH])
        convw = sbuf(st, "convw", [P, CONV_K, QKV_TILES])
        sq_junk = sbuf(st, "sq_junk", [P, 2, P])
        sso_junk = sbuf(st, "sso_junk", [P, 2, P])
        sc = {n: sbuf(st, "sc_" + n, [P, GH, NT]) for n in
              ("beta", "g", "gc", "exp", "nexp", "kdec", "elast", "ssk", "ssq", "cj", "ncj", "rk", "aq", "sso")}
        norm_g = sbuf(st, "norm_g", [P, 1])
        xs = sbuf(st, "xs", [P, 2, HALF + CONV_K - 1])
        th = sbuf(st, "th", [P, HALF])
        spare_at = taken[0]
        vT = sbuf(st, "vT", [P, SEQ])
        chunk_buffers(0)
        gates = vT[0:16, :]
        conv_rows = qT[0][0:CONV_K, :]
        gc_raw = o_flat[64:128, 0:HALF]
        gt = conv[:, :].rearrange("p (a h c) -> p a h c", a=8, h=GH)
        st.close()

        taken[0] = 0
        st = ExitStack()
        bT = sbuf(st, "bT", [P, NK, SEQ])
        st1 = ExitStack()
        kd = sbuf(st1, "kd", [P, 2, P + SEQ])
        vv = sbuf(st1, "vv", [P, 1 + NT, P])
        window = sbuf(st1, "window", [P, 2, 2 * P])
        sinks = sbuf(st1, "sinks", [P, SH])
        after_projection = taken[0]
        raw_at = 4 * (NK + 2 * (NK - 1)) * DM + 512
        stp = ExitStack()
        ws_hi = sbuf(stp, "ws_hi", [P, WR, HALF], F32R)
        ws_lo = sbuf(stp, "ws_lo", [P, WR, HALF], F32R)
        qr = sbuf(stp, "qr", [P, 2, HALF])
        room = sbuf(stp, "room", [P, (spare_at - taken[0]) // 4])
        kv_lo = sbuf(stp, "kv_lo", [P, NK, 2 * P], F32R)
        cosr = sbuf(stp, "cosr", [P, NT, HD])
        sinr = sbuf(stp, "sinr", [P, NT, HD])
        rot = sbuf(stp, "rot", [P, 2, HALF])
        stp.close()
        taken[0] = after_projection
        stz = ExitStack()
        z_hi, z_lo = [None] * 2, [None] * 2
        z_hi[1] = sbuf(stz, "z_hi1", [P, NK, P], F32R)
        z_lo[1] = sbuf(stz, "z_lo1", [P, NK, P], F32R)
        zt = sbuf(stz, "zt", [P, HALF])
        logit = sbuf(stz, "logit", [P, 2, 4, 2 * P])
        prob = sbuf(stz, "prob", [P, 2, 2, 4, P])
        sm = {n: sbuf(stz, "sm_" + n, [P, 2, 4]) for n in ("max", "neg", "sum", "off", "sink", "den", "rden")}
        room1 = sbuf(stz, "room1", [P, (raw_at - 12 * DM - taken[0]) // 4])
        zg = sbuf(stz, "zg", [P, 3, SEQ])
        z_lo[0] = sbuf(stz, "z_lo0", [P, NK, P], F32R)
        room2 = sbuf(stz, "room2", [P, (spare_at - taken[0]) // 4])
        z_raw = sbuf(stz, "z_raw", [P, NK, P])
        z_hi[0] = sbuf(stz, "z_hi0", [P, NK, P], F32R)
        stz.close()
        st1.close()
        st.close()

        taken[0] = 0
        st = ExitStack()
        lng = sbuf(st, "lng", [P, DM])
        lnb = sbuf(st, "lnb", [P, DM])
        xres = sbuf(st, "xres", [P, 2, DM])
        yr = sbuf(st, "yr", [P, 2, DM])
        kv_hi = sbuf(st, "kv_hi", [P, NK, 2 * P], F32R)
        wo_hi, wo_lo = [None] * NK, [None] * NK
        for k in range(1, NK):
            wo_hi[k] = sbuf(st, f"wo_hi{k}", [P, DM], F32R)
        for k in range(1, NK):
            wo_lo[k] = sbuf(st, f"wo_lo{k}", [P, DM], F32R)
        stats = sbuf(st, "stats", [P, 2, 2, 6])
        mv = sbuf(st, "mv", [P, 2, 4])
        ws_raw = sbuf(st, "ws_raw", [P, 2, HALF])
        gap = sbuf(st, "gap", [P, (spare_at - taken[0]) // 4])
        wo_raw = sbuf(st, "wo_raw", [P, 2, DM])
        wo_hi[0] = sbuf(st, "wo_hi0", [P, DM], F32R)
        wo_lo[0] = sbuf(st, "wo_lo0", [P, DM], F32R)
        st.close()

        s_const = sem("s_const")
        s_x = [sem(f"s_x{t}") for t in range(NT)]
        s_small = sem("s_small")
        s_xtr = sem("s_xtr")
        s_xhi = sem("s_xhi")
        s_xlo = sem("s_xlo")
        s_ctr = sem("s_ctr")
        s_cw = sem("s_cw")
        s_wraw = sem("s_wraw")
        s_whi = sem("s_whi")
        s_wlo = sem("s_wlo")
        s_group = sem("s_group")
        s_gev = sem("s_gev")
        s_gtr = sem("s_gtr")
        s_gd = sem("s_gd")
        s_ga = sem("s_ga")
        s_gc = sem("s_gc")
        s_gct = sem("s_gct")
        s_gr = sem("s_gr")
        s_gio = sem("s_gio")
        s_halo = sem("s_halo")
        s_evac = sem("s_evac")
        s_tap = sem("s_tap")
        s_th = sem("s_th")
        s_silu = sem("s_silu")
        s_zth = sem("s_zth")
        s_zt = sem("s_zt")
        s_gated = sem("s_gated")
        s_kd = sem("s_kd")
        s_dve = sem("s_dve")
        s_act = sem("s_act")
        s_tr = sem("s_tr")
        s_sq = sem("s_sq")
        s_sk = sem("s_sk")
        s_tev = sem("s_tev")
        s_ak = sem("s_ak")
        s_rk = sem("s_rk")
        s_vs = sem("s_vs")
        s_gcr = sem("s_gcr")
        s_dp = sem("s_dp")
        s_dt = sem("s_dt")
        s_kk = sem("s_kk")
        s_m = sem("s_m")
        s_pin = sem("s_pin")
        s_pb = sem("s_pb")
        s_pool = sem("s_pool")
        s_inv = sem("s_inv")
        s_pout = sem("s_pout")
        s_xt = sem("s_xt")
        s_xr = sem("s_xr")
        s_lv = sem("s_lv")
        s_ut = sem("s_ut")
        s_xl = sem("s_xl")
        s_ks = sem("s_ks")
        s_qs = sem("s_qs")
        s_resid = sem("s_resid")
        s_oq = sem("s_oq")
        s_y = sem("s_y")
        s_vnew = sem("s_vnew")
        s_su = sem("s_su")
        s_av = sem("s_av")
        s_state = sem("s_state")
        s_o = sem("s_o")
        s_sso = sem("s_sso")
        s_of = sem("s_of")
        s_fs = sem("s_fs")
        s_oscaled = sem("s_oscaled")
        s_ot = sem("s_ot")
        s_otev = sem("s_otev")

        L = []
        for i in range(2):
            L.append({n: sem(f"l{i}_{n}") for n in
                      ("ohi", "olo", "wohi", "wolo", "y", "params", "yev", "st", "sqrt", "dve", "ln",
                       "xtr", "xhi", "xlo")})
            L[i]["x"] = [sem(f"l{i}_x{j}") for j in range(2)]
            L[i]["o"] = [sem(f"l{i}_o{j}") for j in range(2)]
            L[i]["wr"] = [sem(f"l{i}_wr{j}") for j in range(2)]

        q_c = sem("q_const")
        q_small = sem("q_small")
        q_kvraw = sem("q_kvraw")
        q_kvhi = sem("q_kvhi")
        q_kvlo = sem("q_kvlo")
        q_slice = sem("q_slice")
        q_raw = [sem(f"q_raw{i}") for i in range(2)]
        q_hi = sem("q_hi")
        q_lo = sem("q_lo")
        q_group = sem("q_group")
        q_rope = sem("q_rope")
        q_dve = sem("q_dve")
        q_tr = sem("q_tr")
        q_tev = sem("q_tev")
        z_rawd = sem("z_rawd")
        z_his = sem("z_his")
        z_los = sem("z_los")
        z_group = sem("z_group")
        z_th = sem("z_th")
        z_t = sem("z_t")
        s_s = sem("s_s")
        s_logit = sem("s_logit")
        s_neg = sem("s_neg")
        s_e = sem("s_e")
        s_norm = sem("s_norm")
        s_pt = sem("s_pt")
        s_pe0 = sem("s_pe0")
        s_pe1 = sem("s_pe1")
        s_pv = sem("s_pv")
        s_ob = sem("s_ob")
        s_bg = sem("s_bg")

        wa_tiles = wa.rearrange("(k p) n -> p k n", p=P)
        wb_tiles = wb.rearrange("(k p) n -> p k n", p=P)
        kv_raw = ws_raw[:, :, :].rearrange("p a (b n) -> p (a b) n", b=2)
        block = ctx.enter_context(nc.Block())

        def bank_free(eng, g):
            if g < 0:
                eng.wait_ge(s_gev, g + 3)
            elif g < QKV_GROUPS:
                eng.wait_ge(s_evac, g + 1)
            else:
                eng.wait_ge(s_zt, g - QKV_GROUPS + 1)

        def channel_tile(w):
            return (w % 3) * GH + w // 3 if w < QKV_TILES else w

        @block.sync
        def _(sp):
            for t in range(NT):
                sp.dma_start(tok[:, t, :], x[0, t * P:(t + 1) * P, :]).then_inc(s_x[t], 16)
            sp.dma_start(bias2[:, 0, :], a_dt_bias[0].partition_broadcast(P)).then_inc(s_small, 16)
            sp.dma_start(bias2[:, 1, :], a_a_log[0].partition_broadcast(P)).then_inc(s_small, 16)
            sp.dma_start(norm_g[:, :], a_norm_g[0].rearrange("(p a) -> p a", a=1)).then_inc(s_small, 16)
            for i, buf in enumerate((qT[0], kT[0], qT[1])):
                sp.dma_start(buf[0:CONV_K, :], a_conv[0][:, DM * i:DM * (i + 1)]).then_inc(s_small, 16)
            sp.wait_ge(s_gr, 1)
            sp.dma_start(gc_rows.rearrange("r (c j) -> (r c) j", c=4), o_tok[0:64, 0, :]).then_inc(s_gio, 16)
            sp.wait_ge(s_gio, 16)
            sp.wait_ge(s_gr, 2)
            for i in range(2):
                sp.dma_start(gc_raw[32 * i:32 * i + 16, :], gc_rows).then_inc(s_gio, 16)
            for h in range(GH):
                sp.wait_ge(s_m, NT * (h + 1))
                for b in range(4):
                    sp.dma_start(blocks_in[h % 2].rearrange("(c b) j i -> b j c i", b=4)[b],
                                 nT[h % 2][32 * b:32 * b + 32, :, 32 * b:32 * b + 32]).then_inc(s_pin, 16)
                sp.wait_ge(s_pin, 64 * (h + 1))
                sp.dma_start(blocks[:, :, :], blocks_in[h % 2]).then_inc(s_pb, 16)
                sp.wait_ge(s_inv, h + 1)
                sp.dma_start(blocks_out[h % 2], blocks[:, :, :]).then_inc(s_pout, 16)
                sp.wait_ge(s_pout, 16 * (h + 1))
                if h:
                    sp.wait_ge(s_y, NT * h)
                else:
                    sp.wait_ge(s_const, 12)
                for b in range(4):
                    sp.dma_start(xT[32 * b:32 * b + 32, :, 32 * b:32 * b + 32],
                                 blocks_out[h % 2].rearrange("(c b) j i -> b j c i", b=4)[b]).then_inc(s_xt, 16)

            def out_stage(i):
                s = L[i]
                for k in range(NK):
                    if i == 0 and k < 2:
                        sp.wait_ge(s_tr, 2 * GH)
                        sp.wait_ge(s_av, NT * (GH - 1))
                    if i == 1 and k == 0:
                        sp.wait_ge(z_los, NK)
                    if i == 1 and k == 1:
                        sp.wait_ge(z_group, 2 * (NK - 1))
                    if k >= 2:
                        sp.wait_ge(s["wolo"], k - 1)
                    sp.dma_start(wo_raw[:, k % 2, :], w_out[i][k * P:(k + 1) * P, :]).then_inc(s["wr"][k % 2], 16)
                sp.wait_ge(s["olo"], NK)
                sp.dma_start(lng[:, :], ln_g[i].partition_broadcast(P)).then_inc(s["params"], 16)
                sp.dma_start(lnb[:, :], ln_b[i].partition_broadcast(P)).then_inc(s["params"], 16)
                for t in range(NT):
                    if i == 0:
                        if t >= 2:
                            sp.wait_ge(s["yev"], 2 * (t - 1))
                        sp.dma_start(xres[:, t % 2, :], x[0, t * P:(t + 1) * P, :]).then_inc(s["x"][t % 2], 16)
                        if t == 3 or t == NT - 1:
                            b = t // 4
                            if b:
                                sp.wait_ge(q_kvlo, 1)
                            else:
                                sp.wait_ge(s_gated, 2 * GH)
                            sp.dma_start(kv_raw[:, :, :], wb_tiles[:, 4 * b:4 * b + 4, DM:DM + 2 * P])\
                              .then_inc(q_kvraw, 16)
                    else:
                        sp.wait_ge(s["ln"], t + 1)
                        sp.dma_start(out[0, t * P:(t + 1) * P, :], yr[:, t % 2, :]).then_inc(s["o"][t % 2], 16)

            out_stage(0)
            sp.wait_ge(L[0]["y"], NT)
            sp.dma_start(cosr[:, :, :], rope_cos.rearrange("(t p) d -> p t d", p=P)).then_inc(q_small, 16)
            sp.dma_start(sinr[:, :, :], rope_sin.rearrange("(t p) d -> p t d", p=P)).then_inc(q_small, 16)
            sp.dma_start(sinks[:, :], b_sinks[0].partition_broadcast(P)).then_inc(q_small, 16)
            sp.wait_ge(q_kvlo, 2)
            for n in range(SLICES):
                if n >= 2:
                    sp.wait_ge(q_lo, n - 1)
                bl, k = n // NK, n % NK
                sp.dma_start(ws_raw[:, n % 2, :], wb[k * P:(k + 1) * P, HALF * bl:HALF * (bl + 1)])\
                  .then_inc(q_raw[n % 2], 16)
            sp.wait_ge(q_group, NT)
            for j in range(NK):
                if j:
                    sp.wait_ge(z_los, j)
                sp.dma_start(z_raw[:, :, :], wb_tiles[:, :, SWA_Z0 + P * j:SWA_Z0 + P * (j + 1)]).then_inc(z_rawd, 16)
            out_stage(1)
            for j in range(2):
                sp.wait_ge(L[1]["o"][j], 16 * NT // 2)

        @block.gpsimd
        def _(pool):
            steps = Link(pool, s_const)
            steps.next(pool.memset(ident[:, :], 0.0))
            steps.next(pool.memset(tri[:, :], 1.0))
            steps.next(pool.memset(causal[:, :], 0.0))
            steps.next(pool.memset(w_raw[:, :, 16:P], 0.0))
            steps.next(pool.memset(xs[:, 0, 0:CONV_K - 1], 0.0))
            steps.wait()
            steps.next(pool.affine_select(out=ident[:, :], in_=ident[:, :], compare_op=ALU.not_equal, fill=1.0,
                                          base=0, pattern=[[-1, P]], channel_multiplier=1))
            steps.next(pool.affine_select(out=tri[:, :], in_=tri[:, :], compare_op=ALU.is_ge, fill=0.0,
                                          base=0, pattern=[[1, P]], channel_multiplier=-1))
            steps.next(pool.affine_select(out=causal[:, :], in_=causal[:, :], compare_op=ALU.is_ge, fill=NEG,
                                          base=0, pattern=[[1, P]], channel_multiplier=-1))
            for q in range(4):
                steps.next(pool.memset(xT[:, 2 * q:2 * q + 2, :], 0.0))
            inner = Link(pool, s_pool)
            for h in range(GH):
                pool.wait_ge(s_pb, 16 * (h + 1))
                for m in range(30, 0, -1):
                    w = 31 - m
                    part = rank1[:, 0:m * w].rearrange("p (a b) -> p a b", a=m)
                    inner.next(pool.tensor_tensor(part, blocks[:, 0:m, m:m + 1].broadcast_to([32, m, w]),
                                                  blocks[:, m:m + 1, m + 1:32].broadcast_to([32, m, w]), ALU.mult))
                    inner.wait()
                    inner.next(pool.tensor_tensor(blocks[:, 0:m, m + 1:32], blocks[:, 0:m, m + 1:32], part, ALU.add))
                    inner.wait()
                flat = blocks[:, :, :].rearrange("p a b -> p (a b)")
                pool.memset(flat[:, 0:1024:33], 1.0).then_inc(s_inv, 1)
            pool.wait_ge(L[0]["xlo"], 2 * NT)
            steps = Link(pool, q_c)
            steps.next(pool.memset(kd[:, :, 0:P], 0.0))
            steps.next(pool.memset(vv[:, 0, :], 0.0))
            steps.next(pool.memset(window[:, :, :], 0.0))
            steps.wait()
            steps.next(pool.affine_select(out=window[:, :, :], in_=window[:, :, :], compare_op=ALU.is_gt, fill=NEG,
                                          base=0, pattern=[[0, 2], [1, 2 * P]], channel_multiplier=-1))
            steps.wait()
            steps.next(pool.affine_select(out=window[:, :, :], in_=window[:, :, :], compare_op=ALU.is_ge, fill=NEG,
                                          base=P, pattern=[[0, 2], [-1, 2 * P]], channel_multiplier=1))
            steps.wait()
            steps.next(pool.memset(window[:, 0, 0:P], NEG))

            def low_gate(j):
                pool.wait_ge(z_his, j + 1)
                if j == 0:
                    pool.wait_ge(q_lo, SLICES)
                if j >= 2:
                    pool.wait_ge(z_group, 2 * (j - 1))
                pool.tensor_tensor(z_lo[j % 2][:, :, :], z_raw[:, :, :], z_hi[j % 2][:, :, :].bitcast(F32),
                                   ALU.subtract).then_inc(z_los, 1)

            def apply_gate(j):
                pool.wait_ge(s_ob, NT * (j // 2 + 1))
                pool.wait_ge(z_t, 2 * (j + 1))
                pool.tensor_tensor(bT[:, j, :], zg[:, (j + 1) % 3, :], bT[:, j, :], ALU.mult).then_inc(s_bg, 1)

            low_gate(0)
            low_gate(1)
            low_gate(2)
            for j in range(0, NK, 2):
                apply_gate(j)
                apply_gate(j + 1)
                for m in (j + 3, j + 4):
                    if m < NK:
                        low_gate(m)

        @block.tensor
        def _(pe):
            pe.wait_ge(s_const, 8)

            def project(g, q):
                w, b = g // 2, g % 2
                if q == 0:
                    pe.wait_ge(s_whi, w + 2)
                    pe.wait_ge(s_wlo, w + 2)
                    if g >= 0:
                        bank_free(pe, g - 2)
                for i in range(q, q + STEP):
                    k, j = i // PASSES, i % PASSES
                    lhs = (w_hi, w_hi, w_lo)[j][w % 2]
                    rhs = (act_hi, act_lo, act_hi)[j]
                    mm = pe.matmul(ps[:, g % 2, :], lhs[:, k, :], rhs[:, k, HALF * b:HALF * (b + 1)],
                                   start=(i == 0), stop=(i == GROUP - 1))
                if q + STEP == GROUP:
                    mm.then_inc(s_group, 1)

            def turn_input(t):
                pe.wait_ge(s_x[t], 16)
                for b in range(2):
                    n = 2 * t + b
                    if n >= 4:
                        pe.wait_ge(s_xlo, n - 3)
                    for k in range(4):
                        mm = pe.transpose(ps[:, 4 + n % 4, k * P:(k + 1) * P],
                                          tok[:, t, (4 * b + k) * P:(4 * b + k + 1) * P], ident[:, :])
                    mm.then_inc(s_xtr, 1)

            for t in range(NT):
                turn_input(t)
            pe.wait_ge(s_xlo, NT)
            for q in range(0, GROUP, STEP):
                project(-2, q)
            pe.wait_ge(s_small, 96)
            for w in range(QKV_TILES):
                buf = (qT[0], kT[0], qT[1])[w // 8]
                mm = pe.transpose(ps[:, 2, CONV_K * w:CONV_K * (w + 1)], buf[0:CONV_K, (w % 8) * P:(w % 8 + 1) * P],
                                  ident[0:CONV_K, 0:CONV_K])
            mm.then_inc(s_ctr, 1)
            pe.wait_ge(s_xlo, 2 * NT)

            for q in range(0, GROUP, STEP):
                project(-1, q)
            pe.wait_ge(s_gev, 2)
            for c in range(NT):
                mm = pe.transpose(ps[:, 3, 16 * c:16 * (c + 1)], gates[:, c * P:(c + 1) * P], ident[0:16, 0:16])
            mm.then_inc(s_gtr, 1)
            for q in range(0, GROUP, STEP):
                project(0, q)
            pe.wait_ge(s_gd, 3)
            g_all = sc["g"][:, :, :].rearrange("p h c -> p (h c)")
            pe.matmul(ps[:, 3, 128:192], tri[:, :], g_all, start=True, stop=True)
            pe.matmul(ps[:, 3, 192:256], tri[:, P - 1:P].broadcast_to([P, P]), g_all,
                      start=True, stop=True).then_inc(s_gc, 1)

            pe.wait_ge(s_gd, 5)
            pe.transpose(ps[0:64, 3, 256:384], sc["gc"][:, :, :].rearrange("p h c -> p (h c)"), ident[:, :])\
              .then_inc(s_gct, 1)

            def token_major(h, i):
                n = 2 * h + i
                if i == 0:
                    pe.wait_ge(s_silu, 6 * (h + 1))
                if i == 0 and h >= 2:
                    pe.wait_ge(s_xl, 2 * (h - 1))
                if n:
                    pe.wait_ge(s_sk, 4 * n)
                for bank, src in ((7, kT[h % 3]), (5, vT), (6, qT[h % 3])):
                    if bank == 5:
                        if i == 0 and h >= 1:
                            pe.wait_ge(s_m, NT * h)
                        if n:
                            pe.wait_ge(s_tev, n)
                    elif bank == 6 and n:
                        pe.wait_ge(s_sq, 4 * n)
                    if i == 0 and h >= 2 and bank != 7:
                        pe.wait_ge(s_otev, 2 * (h - 2) + bank - 4)
                    for c in range(4):
                        mm = pe.transpose(ps[:, bank, c * P:(c + 1) * P],
                                          src[:, (4 * i + c) * P:(4 * i + c + 1) * P], ident[:, :])
                mm.then_inc(s_tr, 1)

            def scores(h, c):
                if c == 0:
                    pe.wait_ge(s_tev, 2 * h + 2)
                    pe.wait_ge(s_sk, NT * (h + 1))
                    if h == 0:
                        pe.wait_ge(s_gr, 6)
                elif c == 4:
                    pe.wait_ge(s_dp, NT * h + c)
                if c % 4 == 0:
                    row = 2 * h + c // 4
                    pe.matmul(ps[:, 7, :], chosen[64:128, row:row + 1].broadcast_to([64, P]), gc_table,
                              start=True, stop=True).then_inc(s_gcr, 1)
                if c >= 2:
                    pe.wait_ge(s_m, NT * h + c - 1)
                elif c == 1:
                    pe.wait_ge(s_sq, NT * (h + 1))
                bank = 5 + c % 2
                cut = slice(c * P, (c + 1) * P)
                pe.matmul(ps[:, bank, 0:P], kT[h % 3][:, cut], kT[h % 3][:, cut], start=True, stop=True)
                pe.matmul(ps[:, bank, P:2 * P], kT[h % 3][:, cut], qT[h % 3][:, cut],
                          start=True, stop=True).then_inc(s_kk, 1)

            def level(h, i):
                n = nT[h % 2]
                if i == 0:
                    pe.wait_ge(s_xr, h + 1)
                    pe.wait_ge(s_m, NT * min(h + 2, GH))
                    if h >= 1:
                        pe.wait_ge(s_otev, 2 * h)
                elif i == 1:
                    pe.wait_ge(s_ut, 2 * h + 1)
                elif i == 2:
                    pe.wait_ge(s_xl, 2 * h + 1)
                else:
                    pe.wait_ge(s_ut, 2 * h + 2)
                for c in range(NT):
                    if i == 0:
                        for a in (0, 64):
                            b = a + 32
                            mm = pe.matmul(ps[b:b + 32, 6, 32 * c:32 * c + 32], n[a:a + 32, c, b:b + 32],
                                           xr[a:a + 32, c, 0:32], start=True, stop=True)
                    elif i == 1:
                        for a in (0, 64):
                            b = a + 32
                            mm = pe.matmul(ps[a:a + 32, 7, 32 * c:32 * c + 32], uT[b:b + 32, c, 0:32],
                                           xT[b:b + 32, c, b:b + 32], start=True, stop=True)
                        mm = pe.matmul(ps[32:64, 7, 32 * c:32 * c + 32], xT[32:64, c, 32:64], uT[32:64, c, 0:32],
                                       start=True, stop=True)
                    elif i == 2:
                        mm = pe.matmul(ps[64:128, 6, 64 * c:64 * c + 64], n[0:64, c, 64:128], xr[0:64, c, 0:64],
                                       start=True, stop=True)
                    else:
                        mm = pe.matmul(ps[0:64, 7, 64 * c:64 * c + 64], uT[64:128, c, 0:64], xT[64:128, c, 64:128],
                                       start=True, stop=True)
                mm.then_inc(s_lv, 1)

            def with_state(h, c):
                if c == 0:
                    return
                cut = slice(c * P, (c + 1) * P)
                pe.wait_ge(s_state, 7 * h + c)
                pe.wait_ge(s_o, NT * h + c)
                pe.matmul(ps[:, 2, 0:P], kT[h % 3][:, cut], state[:, :], start=True, stop=True).then_inc(s_ks, 1)
                if 7 * h + c - 1 > 0:
                    pe.wait_ge(s_oq, 7 * h + c - 1)
                pe.matmul(ps[:, 3, 0:P], qT[h % 3][:, cut], state[:, :], start=True, stop=True).then_inc(s_qs, 1)

            def solve(h, c):
                if c == 0:
                    pe.wait_ge(s_xl, 2 * h + 2)
                    pe.wait_ge(s_vs, h + 1)
                    rhs = v_tok[h % 2][:, 0, :]
                else:
                    pe.wait_ge(s_resid, 7 * h + c)
                    rhs = resid[:, :]
                if 7 * h + c > 0:
                    pe.wait_ge(s_oq, 7 * h + c)
                pe.matmul(ps[:, 3, P:2 * P], xT[:, c, :], rhs, start=True, stop=True).then_inc(s_y, 1)

            def update(h, c):
                pe.wait_ge(s_vnew, NT * h + c + 1)
                if c == 0 and h >= 1:
                    pe.wait_ge(s_o, NT * h)
                if c < NT - 1:
                    pe.matmul(ps[:, 4, 0:P], k_dec[h % 2][:, c, :], v_new[:, :], start=True, stop=True)\
                      .then_inc(s_su, 1)
                pe.matmul(ps[:, 2, P:2 * P], aT[h % 2][:, c, :], v_new[:, :], start=True, stop=True)\
                  .then_inc(s_av, 1)

            def transpose_out(h):
                pe.wait_ge(s_oscaled, h + 1)
                pe.wait_ge(s_m, NT * min(h + 2, GH))
                for b in range(2):
                    for c in range(4):
                        mm = pe.transpose(ps[:, 5 + b, c * P:(c + 1) * P], o_tok[:, 4 * b + c, :], ident[:, :])
                    mm.then_inc(s_ot, 1)

            def out_step(i, t, k):
                for half in range(2):
                    for j in range(PASSES):
                        lhs = (act_hi, act_hi, act_lo)[j]
                        rhs = (wo_hi, wo_lo, wo_hi)[j][k]
                        mm = pe.matmul(ps[:, OUT_BANKS[t] + half, :], lhs[:, k, t * P:(t + 1) * P],
                                       rhs[:, HALF * half:HALF * (half + 1)],
                                       start=(k == 0 and j == 0), stop=(k == NK - 1 and j == PASSES - 1))
                if k == NK - 1:
                    mm.then_inc(L[i]["y"], 1)

            def out_pair(i, k):
                pe.wait_ge(L[i]["olo"], k + 1)
                pe.wait_ge(L[i]["wolo"], k + 1)
                if i == 0 and k == 0:
                    pe.wait_ge(s_zt, 2 * GH)
                    pe.wait_ge(s_o, NT * GH)
                out_step(i, 0, k)
                out_step(i, 1, k)

            for p, events in enumerate(PLANS):
                for kind, a, b in events:
                    if kind == "mm" and a > 0:
                        project(a, b)
                    elif kind == "W" and a == 0:
                        out_pair(0, 0)
                    elif kind == "T":
                        token_major(p - 1, a)
                    elif kind == "OT":
                        transpose_out(p - 3)
                    elif kind == "M" and a < NT:
                        scores(p - 1, a)
                    elif kind == "L":
                        level(b, a)
                    elif kind == "A":
                        with_state(b, a)
                    elif kind == "B":
                        solve(b, a)
                    elif kind == "C":
                        update(b, a)

            def project_step(n, k):
                bl, t = n // NT, n % NT
                w = (2 * P, HALF, HALF)[bl]
                sl = ((bl - 1) * NK + k) % WR
                hi, lo = (kv_hi[:, k, :], kv_lo[:, k, :]) if bl == 0 else (ws_hi[:, sl, :], ws_lo[:, sl, :])
                if k == 0:
                    if n < 2:
                        pe.wait_ge(L[0]["yev"], 2 * NT)
                        pe.wait_ge(q_kvlo, 2)
                    if bl == 0:
                        pe.wait_ge(L[0]["xlo"], 2 * max(t + 1, NT - 1 if n >= 2 else 0))
                    if n >= 4:
                        pe.wait_ge(q_rope, n - 3)
                if bl >= 1 and t == 0:
                    pe.wait_ge(q_lo, (bl - 1) * NK + k + 1)
                for j in range(PASSES):
                    lhs = (act_hi, act_hi, act_lo)[j]
                    rhs = (hi, lo, hi)[j]
                    mm = pe.matmul(ps[:, TOKEN_BANKS[n % 4], 0:w], lhs[:, k, t * P:(t + 1) * P], rhs,
                                   start=(k == 0 and j == 0), stop=(k == NK - 1 and j == PASSES - 1))
                return mm

            def project_tokens(n):
                for k in range(NK):
                    mm = project_step(n, k)
                mm.then_inc(q_group, 1)

            def out_stage(i):
                s = L[i]

                def turn(t):
                    pe.wait_ge(s["ln"], t + 1)
                    for b in range(2):
                        n = 2 * t + b
                        if n >= 4:
                            pe.wait_ge(s["xlo"], n - 3)
                        elif n >= 2:
                            pe.wait_ge(s["yev"], 6)
                        for k in range(4):
                            mm = pe.transpose(ps[:, 4 + (n + 2) % 4, k * P:(k + 1) * P],
                                              tok[:, t, (4 * b + k) * P:(4 * b + k + 1) * P], ident[:, :])
                        mm.then_inc(s["xtr"], 1)

                before = (None, None, None, 0, 1, 3, 4, 5)

                for k in range(1 - i, NK):
                    out_pair(i, k)
                for t in range(2, NT):
                    if before[t] is not None:
                        pe.wait_ge(s["yev"], 2 * (before[t] + 1))
                    for k in range(NK):
                        out_step(i, t, k)
                    if i == 0:
                        for u in ((0,), (1,), (2, 3), (4,), (5,), (6,))[t - 2]:
                            turn(u)
                if i == 0:
                    project_tokens(0)
                    project_tokens(1)
                    turn(NT - 1)

            out_stage(0)

            def turn_tokens(n):
                pe.wait_ge(q_rope, n + 1)
                if n >= 2:
                    pe.wait_ge(q_tev, n - 1)
                for c in range(2 if n < NT else 4):
                    mm = pe.transpose(ps[:, 2 + n % 2, c * P:(c + 1) * P], qr[:, n % 2, c * P:(c + 1) * P], ident[:, :])
                mm.then_inc(q_tr, 1)

            last = 2 * NT - 1
            for n in range(2, 3 * NT):
                if n == last - 1:
                    for k in range(NK):
                        for m in (n, last):
                            mm = project_step(m, k)
                            if k == NK - 1:
                                mm.then_inc(q_group, 1)
                        if k < NK - 1:
                            mm.then_inc(q_slice, 1)
                elif n != last:
                    project_tokens(n)
                turn_tokens(n - 2)
            for n in (3 * NT - 2, 3 * NT - 1):
                turn_tokens(n)
            pe.wait_ge(q_tev, 3 * NT)
            pe.wait_ge(q_c, 6)

            def logits(u):
                jj, n = u // NT, u % NT
                if u >= 1:
                    pe.wait_ge(s_logit, u)
                for i in range(4):
                    r = 64 * (i % 2)
                    mm = pe.matmul(ps[:, 2 + i % 2, 256 * (i // 2):256 * (i // 2 + 1)],
                                   bT[r:r + 64, 2 * jj + i // 2, n * P:(n + 1) * P],
                                   kd[r:r + 64, jj // 2, n * P:(n + 2) * P], start=True, stop=True)
                mm.then_inc(s_s, 1)

            def project_gate(u):
                g = u // 2
                j, b = g // 2, g % 2
                if u % 2 == 0:
                    pe.wait_ge(z_los, j + 1)
                    if g >= 2:
                        pe.wait_ge(z_t, g - 1)
                for i in range(12 * (u % 2), 12 * (u % 2) + 12):
                    k, q = i // PASSES, i % PASSES
                    lhs = (z_hi, z_hi, z_lo)[q][j % 2]
                    rhs = (act_hi, act_lo, act_hi)[q]
                    mm = pe.matmul(ps[:, g % 2, :], lhs[:, k, :], rhs[:, k, HALF * b:HALF * (b + 1)],
                                   start=(i == 0), stop=(i == GROUP - 1))
                if u % 2:
                    mm.then_inc(z_group, 1)

            def turn_probs(u):
                pe.wait_ge(s_norm, u + 1)
                for w, done in ((0, s_pe0), (1, s_pe1)):
                    if u >= 1:
                        pe.wait_ge(done, u)
                    for i in range(4):
                        mm = pe.transpose(ps[:, 4 + w, i * P:(i + 1) * P], logit[:, u % 2, i, w * P:(w + 1) * P],
                                          ident[:, :])
                    mm.then_inc(s_pt, 1)

            def values(u):
                jj, n = u // NT, u % NT
                kv = jj // 2
                pe.wait_ge(s_pe0, u + 1)
                pe.wait_ge(s_pe1, u + 1)
                if u >= 2:
                    pe.wait_ge(s_ob, u - 1)
                for e in range(2):
                    for w in range(2):
                        mm = pe.matmul(ps[64 * e:64 * e + 64, 6 + u % 2, 0:256].rearrange("p (a q) -> p a q", a=2),
                                       vv[:, n + w, 64 * kv:64 * kv + 64],
                                       prob[:, u % 2, w, e::2, :], start=(w == 0), stop=(w == 1))
                mm.then_inc(s_pv, 1)

            for u in range(UNITS + 2):
                if u < UNITS:
                    logits(u)
                    project_gate(u)
                if 1 <= u <= UNITS:
                    turn_probs(u - 1)
                if u >= 2:
                    values(u - 2)
            out_stage(1)

        @block.scalar
        def _(act):
            own = Link(act, s_act)

            def fetch(w):
                if w >= 0:
                    act.wait_ge(s_wlo, w + 1)
                if w < 0:
                    act.dma_start(w_raw[:, :, 0:16], wa_tiles[:, :, GATE_COL:GDN_IN]).then_inc(s_wraw, 16)
                else:
                    c0 = P * channel_tile(w)
                    act.dma_start(w_raw[:, :, :], wa_tiles[:, :, c0:c0 + P]).then_inc(s_wraw, 16)

            def high(w):
                act.wait_ge(s_wraw, 16 * (w + 2))
                if w >= 1:
                    act.wait_ge(s_group, 2 * w)
                act.activation(w_hi[w % 2][:, :, :], w_raw[:, :, :], ACT.Copy).then_inc(s_whi, 1)

            fetch(-1)
            act.wait_ge(s_const, 5)
            high(-1)
            for n in range(2 * NT):
                act.wait_ge(s_xtr, n + 1)
                t, b = n // 2, n % 2
                act.activation(act_hi[:, 4 * b:4 * b + 4, t * P:(t + 1) * P],
                               ps[:, 4 + n % 4, :].rearrange("p (k q) -> p k q", k=4), ACT.Copy).then_inc(s_xhi, 1)
                if n == 1:
                    fetch(0)
            high(0)
            fetch(1)
            for b in range(2):
                act.wait_ge(s_group, b + 1)
                act.activation(gates[:, HALF * b:HALF * (b + 1)], ps[0:16, b, :], ACT.Copy).then_inc(s_gev, 1)
            act.wait_ge(s_gd, 1)
            act.activation(gt[:, 4], gt[:, 0], ACT.Exp).then_inc(s_ga, 1)
            act.wait_ge(s_gd, 2)
            own.next(act.activation(gt[:, 5], gt[:, 3], ACT.Exp))
            own.wait()
            act.activation(gt[:, 6], gt[:, 5], ACT.Ln, bias=1.0).then_inc(s_ga, 1)
            act.activation(bias2[:, 1, :], bias2[:, 1, :], ACT.Exp).then_inc(s_ga, 1)
            act.wait_ge(s_gd, 6)
            act.activation(sc["exp"][:, :, :], sc["gc"][:, :, :], ACT.Exp).then_inc(s_ga, 1)
            act.activation(sc["kdec"][:, :, :], gt[:, 1], ACT.Exp).then_inc(s_ga, 1)
            act.activation(sc["elast"][:, :, :], gt[:, 0], ACT.Exp).then_inc(s_ga, 1)

            def evacuate(g):
                b = g % 2
                act.wait_ge(s_group, g + 3)
                if g >= QKV_GROUPS:
                    if g == QKV_GROUPS:
                        act.wait_ge(s_silu, QKV_GROUPS)
                    else:
                        act.wait_ge(s_zt, g - QKV_GROUPS)
                    act.activation(th[:, :], ps[:, b, :], ACT.Tanh, scale=0.5).then_inc(s_zth, 1)
                    return
                if g >= 2:
                    act.wait_ge(s_tap, g - 1)
                    act.wait_ge(s_halo, g // 2)
                if b:
                    act.wait_ge(s_evac, g)
                    act.activation(xs[:, 1, 0:CONV_K - 1], xs[:, 0, HALF:HALF + CONV_K - 1], ACT.Copy)\
                       .then_inc(s_halo, 1)
                act.activation(xs[:, b, CONV_K - 1:], ps[:, b, :], ACT.Copy).then_inc(s_evac, 1)

            def gate_tanh(g):
                act.wait_ge(s_tap, g + 1)
                if g:
                    act.wait_ge(s_silu, g)
                act.activation(th[:, :], conv[:, :], ACT.Tanh).then_inc(s_th, 1)

            def token_major(h, i):
                act.wait_ge(s_tr, 2 * h + i + 1)
                if h >= 2:
                    act.wait_ge(s_av, NT * (h - 1))
                act.activation(v_tok[h % 2][:, 4 * i:4 * i + 4, :],
                               ps[:, 5, :].rearrange("p (c q) -> p c q", c=4), ACT.Copy).then_inc(s_tev, 1)
                for bank, slot, out_sum, done in ((7, 1, "ssk", s_sk), (6, 0, "ssq", s_sq)):
                    if bank == 7:
                        act.wait_ge(s_kd, 2 * h + i + 1)
                    for q in range(4):
                        c = 4 * i + q
                        if NT * h + c:
                            act.wait_ge(done, NT * h + c)
                        act.activation(sq_junk[:, slot, :], ps[:, bank, q * P:(q + 1) * P], ACT.Square,
                                       accum_out=sc[out_sum][:, h, c:c + 1]).then_inc(done, 1)

            def squares(h, c):
                act.wait_ge(s_o, NT * h + c + 1)
                if NT * h + c >= 2:
                    act.wait_ge(s_sso, NT * h + c - 1)
                act.activation(sso_junk[:, c % 2, :], o_tok[:, c, :], ACT.Square, accum_out=sc["sso"][:, h, c:c + 1])\
                   .then_inc(s_sso, 1)

            def high_out(i, k):
                if i == 0:
                    act.wait_ge(s_group, 2 * TILES + 2)
                    act.wait_ge(s_gated, 2 * (k + 1))
                else:
                    act.wait_ge(z_group, 2 * NK)
                    act.wait_ge(s_bg, k + 1)
                act.activation(act_hi[:, k, :], (tok, bT)[i][:, k, :], ACT.Copy).then_inc(L[i]["ohi"], 1)

            def high_wo(i, k):
                act.wait_ge(L[i]["wr"][k % 2], 16 * (k // 2 + 1))
                if k == 1 and i == 0:
                    act.wait_ge(s_av, NT * GH)
                elif k == 1:
                    act.wait_ge(s_pv, UNITS)
                act.activation(wo_hi[k][:, :], wo_raw[:, k % 2, :], ACT.Copy).then_inc(L[i]["wohi"], 1)

            for p, events in enumerate(SCALAR_PLANS):
                h, o = p - 1, p - 3
                for kind, a, b in events:
                    r = b
                    if kind == "W":
                        high_out(0, a)
                        high_wo(0, a)
                    if kind == "end":
                        evacuate(a)
                    elif kind == "piece" and a < QKV_GROUPS and b == 3:
                        gate_tanh(a)
                    elif kind == "weights":
                        high(a)
                    elif kind == "fetch":
                        fetch(a)
                    elif kind == "T":
                        token_major(h, a)
                    elif kind == "OF":
                        if o >= 0:
                            act.wait_ge(s_of, o + 1)
                            act.activation(sc["sso"][:, o, :], sc["sso"][:, o, :], ACT.Sqrt).then_inc(s_fs, 1)
                        if o + 1 < GH:
                            act.wait_ge(s_ak, o + 2)
                            act.activation(sc["rk"][:, o + 1, :], sc["rk"][:, o + 1, :], ACT.Sqrt).then_inc(s_rk, 1)
                    elif kind == "OT":
                        for q in range(2):
                            act.wait_ge(s_ot, 2 * o + q + 1)
                            act.activation(tok[:, o, HALF * q:HALF * (q + 1)], ps[:, 5 + q, :], ACT.Copy)\
                               .then_inc(s_otev, 1)
                    elif kind == "M":
                        if a < NT:
                            act.wait_ge(s_dp, NT * h + a + 1)
                            act.activation(decay[a % 2][:, :], decay[a % 2][:, :], ACT.Exp).then_inc(s_dt, 1)
                    elif kind == "L" and a == 0:
                        act.wait_ge(s_lv, 4 * r + 1)
                        src = ps[:, 6, 0:256].rearrange("p (c j) -> p c j", c=NT)
                        act.activation(uT[32:64, :, 0:32], src[32:64], ACT.Copy)
                        act.activation(uT[96:128, :, 0:32], src[96:128], ACT.Copy).then_inc(s_ut, 1)
                    elif kind == "L" and a == 2:
                        act.wait_ge(s_lv, 4 * r + 3)
                        act.activation(uT[64:128, :, :], ps[64:128, 6, :].rearrange("p (c j) -> p c j", c=NT),
                                       ACT.Copy).then_inc(s_ut, 1)
                    elif kind == "A" and a >= 1:
                        act.wait_ge(s_qs, 7 * r + a)
                        act.activation(q_state[:, :], ps[:, 3, 0:P], ACT.Copy, scale=sc["exp"][:, r, a:a + 1])\
                           .then_inc(s_oq, 1)
                        squares(r, a - 1)
                    elif kind == "B":
                        act.wait_ge(s_y, NT * r + a + 1)
                        act.activation(v_new[:, :], ps[:, 3, P:2 * P], ACT.Copy, scale=sc["cj"][:, r, a:a + 1])\
                           .then_inc(s_vnew, 1)
                    elif kind == "C" and a == NT - 1:
                        squares(r, a)

            def out_stage(i):
                s = L[i]
                for k in range(NK):
                    if k >= EARLY[i]:
                        high_out(i, k)
                        high_wo(i, k)

                def high_x(t):
                    for b in range(2):
                        n = 2 * t + b
                        act.wait_ge(s["xtr"], n + 1)
                        act.activation(act_hi[:, 4 * b:4 * b + 4, t * P:(t + 1) * P],
                                       ps[:, 4 + (n + 2) % 4, :].rearrange("p (k q) -> p k q", k=4), ACT.Copy)\
                           .then_inc(s["xhi"], 1)

                for t in range(NT):
                    if i == 0 and t in (5, 7):
                        b = t // 2 - 2
                        act.wait_ge(q_kvraw, 16 * (b + 1))
                        act.activation(kv_hi[:, 4 * b:4 * b + 4, :], kv_raw[:, :, :], ACT.Copy).then_inc(q_kvhi, 1)
                    act.wait_ge(s["st"], t + 1)
                    act.activation(mv[:, t % 2, 3:4], mv[:, t % 2, 2:3], ACT.Sqrt).then_inc(s["sqrt"], 1)
                    if i == 0 and t >= 1:
                        high_x(t - 1)
                if i == 0:
                    high_x(NT - 1)

            out_stage(0)

            def high_gate(j):
                act.wait_ge(z_rawd, 16 * (j + 1))
                if j >= 2:
                    act.wait_ge(z_group, 2 * (j - 1))
                act.activation(z_hi[j % 2][:, :, :], z_raw[:, :, :], ACT.Copy).then_inc(z_his, 1)

            def high_slice(n):
                act.wait_ge(q_raw[n % 2], 16 * (n // 2 + 1))
                if n >= WR:
                    act.wait_ge(q_slice, n - WR + 1)
                act.activation(ws_hi[:, n % WR, :], ws_raw[:, n % 2, :], ACT.Copy).then_inc(q_hi, 1)

            for n in range(3 * NT):
                bl, t = n // NT, n % NT
                for m in slices_before(n, 12):
                    high_slice(m)
                if n == GATE_FROM:
                    high_gate(0)
                act.wait_ge(q_tr, n + 1)
                if bl == 0:
                    act.activation(kd[:, :, (t + 1) * P:(t + 2) * P],
                                   ps[:, 2 + n % 2, 0:256].rearrange("p (a q) -> p a q", a=2), ACT.Copy)\
                       .then_inc(q_tev, 1)
                else:
                    act.activation(bT[:, 4 * (bl - 1):4 * bl, t * P:(t + 1) * P],
                                   ps[:, 2 + n % 2, :].rearrange("p (a q) -> p a q", a=4), ACT.Copy)\
                       .then_inc(q_tev, 1)

            for u in range(UNITS + 2):
                if u < UNITS:
                    act.wait_ge(s_neg, u + 1)
                    for i in range(4):
                        act.activation(logit[:, u % 2, i, :], logit[:, u % 2, i, :], ACT.Exp,
                                       bias=sm["neg"][:, u % 2, i:i + 1], accum_out=sm["sum"][:, u % 2, i:i + 1])
                    act.activation(sm["sink"][:, u % 2, :], sm["off"][:, u % 2, :], ACT.Exp).then_inc(s_e, 1)
                if 1 <= u <= UNITS:
                    v = u - 1
                    act.wait_ge(s_pt, 2 * v + 1)
                    if v >= 2:
                        act.wait_ge(s_pv, v - 1)
                    act.activation(prob[:, v % 2, 0], ps[:, 4, :].rearrange("p (i q) -> p i q", i=4), ACT.Copy)\
                       .then_inc(s_pe0, 1)
                if u < UNITS and u % 2:
                    g = u // 2
                    act.wait_ge(z_group, g + 1)
                    if g:
                        act.wait_ge(z_t, g)
                    act.activation(zt[:, :], ps[:, g % 2, :], ACT.Tanh, scale=0.5).then_inc(z_th, 1)
                if u % 4 == 2 and u // 4 + 1 < NK:
                    high_gate(u // 4 + 1)
                if u == UNITS:
                    high_out(1, 0)
                    high_wo(1, 0)
            out_stage(1)

        @block.vector
        def _(dve):
            own = Link(dve, s_dve)

            def low(w):
                dve.wait_ge(s_whi, w + 2)
                dve.tensor_tensor(w_lo[w % 2][:, :, :], w_raw[:, :, :], w_hi[w % 2][:, :, :].bitcast(F32),
                                  ALU.subtract).then_inc(s_wlo, 1)

            low(-1)
            for n in range(2 * NT):
                dve.wait_ge(s_xhi, n + 1)
                t, b = n // 2, n % 2
                cut = (slice(None), slice(4 * b, 4 * b + 4), slice(t * P, (t + 1) * P))
                dve.tensor_tensor(act_lo[cut], ps[:, 4 + n % 4, :].rearrange("p (k q) -> p k q", k=4),
                                  act_hi[cut].bitcast(F32), ALU.subtract).then_inc(s_xlo, 1)
            low(0)
            dve.wait_ge(s_ctr, 1)
            dve.tensor_scalar(convw[:, :, :], ps[:, 2, 0:CONV_K * QKV_TILES].rearrange("p (w k) -> p k w", k=CONV_K),
                              0.5, None, ALU.mult).then_inc(s_cw, 1)
            own.next(dve.tensor_scalar(norm_g[:, :], norm_g[:, :], 0.5, None, ALU.mult))
            dve.wait_ge(s_gtr, 1)
            lg = ps[:, 3, 0:P].rearrange("p (c j) -> p j c", c=NT)
            own.next(dve.tensor_tensor(gt[:, 1], lg[:, GH:2 * GH, :],
                                       bias2[:, 0, :].unsqueeze(2).broadcast_to([P, GH, NT]), ALU.add))
            dve.tensor_scalar(gt[:, 0], lg[:, 0:GH, :], -1.0, 80.0, ALU.mult, ALU.min).then_inc(s_gd, 1)
            own.wait()
            own.next(dve.tensor_scalar(gt[:, 2], gt[:, 1], -1.0, None, ALU.mult))
            own.wait()
            dve.tensor_tensor(gt[:, 3], gt[:, 1], gt[:, 2], ALU.min).then_inc(s_gd, 1)
            dve.wait_ge(s_ga, 3)
            own.next(dve.scalar_tensor_tensor(gt[:, 2], gt[:, 1], 0.0, gt[:, 6], ALU.max, ALU.add))
            own.next(dve.tensor_scalar(gt[:, 7], gt[:, 4], 1.0, None, ALU.add))
            own.wait()
            dve.scalar_tensor_tensor(sc["g"][:, :, :], gt[:, 2], -1.0,
                                     bias2[:, 1, :].unsqueeze(2).broadcast_to([P, GH, NT]), ALU.mult, ALU.mult)\
               .then_inc(s_gd, 1)
            own.next(dve.reciprocal(sc["beta"][:, :, :], gt[:, 7]))
            dve.wait_ge(s_gc, 1)
            gcp = ps[:, 3, 128:192].rearrange("p (h c) -> p h c", h=GH)
            glp = ps[:, 3, 192:256].rearrange("p (h c) -> p h c", h=GH)
            dve.tensor_copy(sc["gc"][:, :, :], gcp).then_inc(s_gd, 1)
            dve.tensor_copy(gt[:, 0], glp).then_inc(s_gd, 1)
            dve.wait_ge(s_gd, 5)
            dve.tensor_tensor(gt[:, 1], gt[:, 0], sc["gc"][:, :, :], ALU.subtract).then_inc(s_gd, 1)
            dve.wait_ge(s_ga, 6)
            own.next(dve.tensor_scalar(sc["nexp"][:, :, :], sc["exp"][:, :, :], -1.0, None, ALU.mult))
            dve.wait_ge(s_gct, 1)
            dve.tensor_copy(o_tok[0:64, 0, :], ps[0:64, 3, 256:384]).then_inc(s_gr, 1)
            dve.memset(gc_raw, 0.0).then_inc(s_gr, 1)

            def split_rows():
                dve.wait_ge(s_gio, 48)
                dve.tensor_copy(gc_table, gc_raw).then_inc(s_gr, 1)
                dve.wait_ge(s_gr, 3)
                dve.tensor_tensor(gc_raw[32:64, :], gc_raw[32:64, :], gc_table[32:64, :].bitcast(F32),
                                  ALU.subtract).then_inc(s_gr, 1)
                dve.wait_ge(s_gr, 4)
                dve.tensor_copy(gc_table[32:64, :], gc_raw[32:64, :]).then_inc(s_gr, 1)
                dve.wait_ge(s_const, 9)
                dve.tensor_tensor(chosen[64:128, :], ident[64:128, 64:80], ident[64:128, 96:112], ALU.add)\
                   .then_inc(s_gr, 1)

            dve.wait_ge(s_cw, 1)

            def piece(g, k):
                w, b = g // 2, g % 2
                if g >= QKV_GROUPS:
                    zacc = xs[:, b, CONV_K - 1:]
                    z = g - QKV_GROUPS
                    if k == 0:
                        dve.wait_ge(s_zth, z + 1)
                        dve.wait_ge(s_tap, QKV_GROUPS)
                        if z >= 2:
                            dve.wait_ge(s_gated, z - 1)
                        dve.scalar_tensor_tensor(zacc, th[:, :], 1.0, ps[:, b, :], ALU.add, ALU.mult).then_inc(s_zt, 1)
                    else:
                        dve.wait_ge(s_zt, z + 1)
                        dve.wait_ge(s_otev, 2 * (z // 2) + 2)
                        dst = tok[:, z // 2, HALF * b:HALF * (b + 1)]
                        dve.scalar_tensor_tensor(dst, zacc, norm_g[:, 0:1], dst, ALU.mult, ALU.mult)\
                           .then_inc(s_gated, 1)
                    return
                h = g // 6
                tile = channel_tile(w)
                if k == 0:
                    dve.wait_ge(s_evac, g + 1)
                    if g:
                        dve.wait_ge(s_silu, g)
                    if b:
                        dve.wait_ge(s_halo, g // 2 + 1)
                    own.next(dve.tensor_scalar(conv[:, :], xs[:, b, 0:HALF], convw[:, 0, tile:tile + 1], None, ALU.mult))
                elif k < CONV_K:
                    own.wait()
                    ins = dve.scalar_tensor_tensor(conv[:, :], xs[:, b, k:k + HALF], convw[:, k, tile:tile + 1], conv[:, :],
                                                   ALU.mult, ALU.add)
                    if k == CONV_K - 1:
                        ins.then_inc(s_tap, 1)
                    else:
                        own.next(ins)
                else:
                    dve.wait_ge(s_th, g + 1)
                    kind = w % 3
                    if kind == 2:
                        if h >= 1:
                            dve.wait_ge(s_tr, 2 * h)
                        dst = vT
                    else:
                        if h >= 3:
                            dve.wait_ge(s_y, NT * (h - 2))
                        dst = (qT, kT)[kind][h % 3]
                    dve.scalar_tensor_tensor(dst[:, HALF * b:HALF * (b + 1)], th[:, :], 1.0, conv[:, :],
                                             ALU.add, ALU.mult).then_inc(s_silu, 1)

            def scalars(h):
                dve.wait_ge(s_sk, NT * (h + 1))
                dve.tensor_scalar(sc["rk"][:, h, :], sc["ssk"][:, h, :], EPS, None, ALU.add).then_inc(s_ak, 1)
                dve.wait_ge(s_ak, h + 1)
                own.next(dve.tensor_scalar(sc["ssk"][:, h, :], sc["ssk"][:, h, :], EPS, None, ALU.add))
                own.wait()
                own.next(dve.reciprocal(sc["ssk"][:, h, :], sc["ssk"][:, h, :]))
                own.wait()
                own.next(dve.tensor_tensor(sc["cj"][:, h, :], sc["ssk"][:, h, :], sc["beta"][:, h, :], ALU.mult))
                own.wait()
                own.next(dve.tensor_scalar(sc["ncj"][:, h, :], sc["cj"][:, h, :], -1.0, None, ALU.mult))

            def exponents(h, c):
                dve.wait_ge(s_gcr, 2 * h + c // 4 + 1)
                if NT * h + c >= 2:
                    dve.wait_ge(s_m, NT * h + c - 1)
                dve.scalar_tensor_tensor(decay[c % 2][:, :], ps[:, 7, P * (c % 4):P * (c % 4 + 1)], sc["gc"][:, h, c:c + 1], causal[:, :],
                                         ALU.subtract, ALU.min).then_inc(s_dp, 1)

            def matrices(h, c):
                dve.wait_ge(s_dt, NT * h + c + 1)
                dve.wait_ge(s_kk, NT * h + c + 1)
                bank = 5 + c % 2
                if c == 0:
                    own.wait()
                own.next(dve.scalar_tensor_tensor(nT[h % 2][:, c, :], ps[:, bank, 0:P], sc["ncj"][:, h, c:c + 1],
                                                  decay[c % 2][:, :], ALU.mult, ALU.mult))
                dve.tensor_tensor(aT[h % 2][:, c, :], ps[:, bank, P:2 * P], decay[c % 2][:, :], ALU.mult)\
                   .then_inc(s_m, 1)

            def low_out(i, k):
                dve.wait_ge(L[i]["ohi"], k + 1)
                dve.tensor_tensor(act_lo[:, k, :], (tok, bT)[i][:, k, :], act_hi[:, k, :].bitcast(F32), ALU.subtract)\
                   .then_inc(L[i]["olo"], 1)

            def low_wo(i, k):
                dve.wait_ge(L[i]["wohi"], k + 1)
                if k >= NK - 2:
                    dve.wait_ge((s_gated, s_bg)[i], (2 * GH, NK)[i])
                dve.tensor_tensor(wo_lo[k][:, :], wo_raw[:, k % 2, :], wo_hi[k][:, :].bitcast(F32), ALU.subtract)\
                   .then_inc(L[i]["wolo"], 1)

            for p, events in enumerate(VECTOR_PLANS):
                h, o = p - 1, p - 3
                for kind, a, b in events:
                    r = b
                    if kind == "W":
                        low_out(0, a)
                        low_wo(0, a)
                    if kind == "piece":
                        if (a, b) == (1, 0):
                            split_rows()
                        piece(a, b)
                    elif kind == "low":
                        low(a)
                    elif kind == "OF":
                        if o >= 0:
                            dve.wait_ge(s_sso, NT * (o + 1))
                            dve.scalar_tensor_tensor(sc["sso"][:, o, :], sc["sso"][:, o, :], 1.0 / P,
                                                     sc["aq"][:, o, :], ALU.mult, ALU.add).then_inc(s_of, 1)
                    elif kind == "T":
                        dve.wait_ge(s_tr, 2 * h + a + 1)
                        if h >= 2:
                            dve.wait_ge(s_av, NT * (h - 1))
                        dve.tensor_tensor(k_dec[h % 2][:, 4 * a:4 * a + 4, :],
                                          ps[:, 7, :].rearrange("p (c q) -> p c q", c=4),
                                          sc["kdec"][:, h, 4 * a:4 * a + 4].unsqueeze(2).broadcast_to([P, 4, P]),
                                          ALU.mult).then_inc(s_kd, 1)
                    elif kind == "VS":
                        v = p - 2
                        dve.wait_ge(s_rk, v + 1)
                        dve.tensor_tensor(v_tok[v % 2][:, :, :], v_tok[v % 2][:, :, :],
                                          sc["rk"][:, v, :].unsqueeze(2).broadcast_to([P, NT, P]), ALU.mult)\
                           .then_inc(s_vs, 1)
                    elif kind == "OS":
                        dve.wait_ge(s_fs, o + 1)
                        own.next(dve.reciprocal(sc["aq"][:, o, :], sc["sso"][:, o, :]))
                        own.wait()
                        dve.tensor_tensor(o_tok[:, :, :], o_tok[:, :, :],
                                          sc["aq"][:, o, :].unsqueeze(2).broadcast_to([P, NT, P]), ALU.mult)\
                           .then_inc(s_oscaled, 1)
                    elif kind == "M":
                        if a == 0:
                            scalars(h)
                        if a == NT:
                            dve.wait_ge(s_sq, NT * (h + 1))
                            own.next(dve.tensor_scalar(sc["aq"][:, h, :], sc["ssq"][:, h, :], EPS, P * EPS,
                                                       ALU.add, ALU.mult))
                        if a < NT:
                            exponents(h, a)
                        if a >= 1:
                            matrices(h, a - 1)
                    elif kind == "X":
                        dve.wait_ge(s_xt, 64 * (r + 1))
                        if r >= 1:
                            dve.wait_ge(s_ot, 2 * r)
                        dve.memset(xr[0:32, :, 32:64], 0.0)
                        dve.transpose(xr[0:32, :, 0:32], xT[0:32, :, 0:32])
                        dve.transpose(xr[32:64, :, 32:64], xT[32:64, :, 32:64])
                        dve.transpose(xr[64:96, :, 0:32], xT[64:96, :, 64:96]).then_inc(s_xr, 1)
                    elif kind == "L" and a == 1:
                        dve.wait_ge(s_lv, 4 * r + 2)
                        src = ps[:, 7, 0:256].rearrange("p (c j) -> p c j", c=NT)
                        dve.tensor_copy(xT[0:32, :, 32:64], src[0:32])
                        dve.tensor_copy(xT[64:96, :, 96:128], src[64:96])
                        dve.tensor_copy(xr[32:64, :, 0:32], src[32:64]).then_inc(s_xl, 1)
                    elif kind == "L" and a == 3:
                        dve.wait_ge(s_lv, 4 * r + 4)
                        dve.tensor_copy(xT[0:64, :, 64:128], ps[0:64, 7, :].rearrange("p (c j) -> p c j", c=NT))\
                           .then_inc(s_xl, 1)
                    elif kind == "A" and a >= 1:
                        dve.wait_ge(s_ks, 7 * r + a)
                        if a == 1:
                            dve.wait_ge(s_vs, r + 1)
                        dve.scalar_tensor_tensor(resid[:, :], ps[:, 2, 0:P], sc["nexp"][:, r, a:a + 1],
                                                 v_tok[r % 2][:, a, :], ALU.mult, ALU.add).then_inc(s_resid, 1)
                    elif kind == "C":
                        if a < NT - 1:
                            dve.wait_ge(s_su, 7 * r + a + 1)
                            if a == 0:
                                dve.tensor_copy(state[:, :], ps[:, 4, 0:P]).then_inc(s_state, 1)
                            else:
                                dve.wait_ge(s_state, 7 * r + a)
                                dve.scalar_tensor_tensor(state[:, :], state[:, :], sc["elast"][:, r, a:a + 1],
                                                         ps[:, 4, 0:P], ALU.mult, ALU.add).then_inc(s_state, 1)
                        dve.wait_ge(s_av, NT * r + a + 1)
                        if a == 0:
                            dve.tensor_copy(o_tok[:, 0, :], ps[:, 2, P:2 * P]).then_inc(s_o, 1)
                        else:
                            dve.wait_ge(s_oq, 7 * r + a)
                            dve.tensor_tensor(o_tok[:, a, :], ps[:, 2, P:2 * P], q_state[:, :], ALU.add)\
                               .then_inc(s_o, 1)

            def out_stage(i):
                s = L[i]
                own = Link(dve, s["dve"])
                for k in range(NK):
                    if k >= EARLY[i]:
                        low_out(i, k)
                        low_wo(i, k)

                def low_x(t):
                    for b in range(2):
                        n = 2 * t + b
                        dve.wait_ge(s["xhi"], n + 1)
                        cut = (slice(None), slice(4 * b, 4 * b + 4), slice(t * P, (t + 1) * P))
                        dve.tensor_tensor(act_lo[cut], ps[:, 4 + (n + 2) % 4, :].rearrange("p (k q) -> p k q", k=4),
                                          act_hi[cut].bitcast(F32), ALU.subtract).then_inc(s["xlo"], 1)

                dve.wait_ge(s["params"], 32)
                for t in range(NT):
                    if i == 0 and t in (5, 7):
                        b = t // 2 - 2
                        dve.wait_ge(q_kvhi, b + 1)
                        dve.wait_ge(s["wolo"], NK)
                        dve.tensor_tensor(kv_lo[:, 4 * b:4 * b + 4, :], kv_raw[:, :, :],
                                          kv_hi[:, 4 * b:4 * b + 4, :].bitcast(F32), ALU.subtract).then_inc(q_kvlo, 1)
                    q = t % 2
                    dve.wait_ge(s["y"], t + 1)
                    if i == 0:
                        dve.wait_ge(s["x"][q], 16 * (t // 2 + 1))
                    elif t >= 2:
                        dve.wait_ge(s["o"][q], 16 * (t // 2))
                    if t:
                        dve.wait_ge(s["ln"], t)
                    x_old = xres[:, q, :] if i == 0 else tok[:, t, :]
                    for half in range(2):
                        cut = slice(HALF * half, HALF * (half + 1))
                        dve.scalar_tensor_tensor(yr[:, q, cut], x_old[:, cut], ALPHA, ps[:, OUT_BANKS[t] + half, :],
                                                 ALU.mult, ALU.add).then_inc(s["yev"], 1)
                    for half in range(2):
                        dve.wait_ge(s["yev"], 2 * t + half + 1)
                        own.next(dve.bn_stats(stats[:, q, half, :], yr[:, q, HALF * half:HALF * (half + 1)]))
                    own.wait()
                    own.next(dve.bn_aggr(mv[:, q, 0:2], stats[:, q, :, :].rearrange("p a b -> p (a b)")))
                    own.wait()
                    dve.tensor_scalar(mv[:, q, 2:3], mv[:, q, 1:2], LN_EPS, None, ALU.add).then_inc(s["st"], 1)
                    dve.wait_ge(s["sqrt"], t + 1)
                    own.next(dve.reciprocal(mv[:, q, 3:4], mv[:, q, 3:4]))
                    own.wait()
                    own.next(dve.tensor_scalar(yr[:, q, :], yr[:, q, :], mv[:, q, 0:1], mv[:, q, 3:4],
                                               ALU.subtract, ALU.mult))
                    own.wait()
                    own.next(dve.tensor_tensor(yr[:, q, :], yr[:, q, :], lng[:, :], ALU.mult))
                    own.wait()
                    dst = tok[:, t, :] if i == 0 else yr[:, q, :]
                    dve.tensor_tensor(dst, yr[:, q, :], lnb[:, :], ALU.add).then_inc(s["ln"], 1)
                    if i == 0 and t >= 1:
                        low_x(t - 1)
                if i == 0:
                    low_x(NT - 1)

            out_stage(0)
            own = Link(dve, q_dve)

            def low_slice(n):
                dve.wait_ge(q_hi, n + 1)
                dve.tensor_tensor(ws_lo[:, n % WR, :], ws_raw[:, n % 2, :], ws_hi[:, n % WR, :].bitcast(F32),
                                  ALU.subtract).then_inc(q_lo, 1)

            dve.wait_ge(q_small, 48)
            for n in range(3 * NT):
                bl, t = n // NT, n % NT
                for m in slices_before(n, 14):
                    low_slice(m)
                dve.wait_ge(q_group, n + 1)
                if n >= 2:
                    dve.wait_ge(q_tr, n - 1)
                heads = KVH if bl == 0 else 8
                w = heads * HD
                bank = TOKEN_BANKS[n % 4]
                src = ps[:, bank, 0:w].rearrange("p (h d) -> p h d", h=heads)
                a = rot[:, 0, 0:w].rearrange("p (h d) -> p h d", h=heads)
                b = rot[:, 1, 0:w].rearrange("p (h d) -> p h d", h=heads)
                cs = cosr[:, t:t + 1, :].broadcast_to([P, heads, HD])
                lo_sin = sinr[:, t:t + 1, 0:HD // 2].broadcast_to([P, heads, HD // 2])
                hi_sin = sinr[:, t:t + 1, HD // 2:HD].broadcast_to([P, heads, HD // 2])
                if n:
                    dve.wait_ge(q_rope, n)
                own.next(dve.tensor_tensor(a, src, cs, ALU.mult))
                own.next(dve.tensor_tensor(b[:, :, 0:HD // 2], src[:, :, HD // 2:HD], lo_sin, ALU.mult))
                own.next(dve.tensor_tensor(b[:, :, HD // 2:HD], src[:, :, 0:HD // 2], hi_sin, ALU.mult))
                if bl == 0:
                    own.next(dve.tensor_copy(vv[:, t + 1, :], ps[:, bank, P:2 * P]))
                own.wait()
                if bl == 0:
                    dst = qr[:, n % 2, 0:2 * w].rearrange("p (h e d) -> p h e d", h=KVH, e=2)
                    own.next(dve.tensor_tensor(dst[:, :, 0, :], a, b, ALU.add))
                    dve.tensor_tensor(dst[:, :, 1, :], a, b, ALU.add).then_inc(q_rope, 1)
                else:
                    dve.tensor_tensor(qr[:, n % 2, :].rearrange("p (h d) -> p h d", h=heads), a, b, ALU.add)\
                       .then_inc(q_rope, 1)

            dve.wait_ge(q_c, 6)
            for u in range(UNITS + 2):
                if u < UNITS:
                    jj, n, q = u // NT, u % NT, u % 2
                    dve.wait_ge(s_s, u + 1)
                    if u >= 2:
                        dve.wait_ge(s_pt, 2 * (u - 1))
                        dve.wait_ge(s_neg, u - 1)
                    for i in range(4):
                        head = 4 * jj + i
                        ins = dve.tensor_tensor_reduce(logit[:, q, i, :],
                                                       ps[:, 2 + i % 2, 256 * (i // 2):256 * (i // 2 + 1)],
                                                       window[:, min(n, 1), :], SCALE, sinks[:, head:head + 1],
                                                       ALU.add, ALU.max, sm["max"][:, q, i:i + 1])
                        if i == 3:
                            ins.then_inc(s_logit, 1)
                        else:
                            own.next(ins)
                    own.wait()
                    dve.wait_ge(s_logit, u + 1)
                    own.next(dve.tensor_scalar(sm["neg"][:, q, :], sm["max"][:, q, :], -1.0, None, ALU.mult))
                    dve.tensor_tensor(sm["off"][:, q, :], sinks[:, 4 * jj:4 * jj + 4], sm["max"][:, q, :],
                                      ALU.subtract).then_inc(s_neg, 1)
                if 1 <= u <= UNITS:
                    v = u - 1
                    q = v % 2
                    dve.wait_ge(s_pt, 2 * v + 2)
                    if v >= 2:
                        dve.wait_ge(s_pv, v - 1)
                    dve.tensor_copy(prob[:, q, 1], ps[:, 5, :].rearrange("p (i q) -> p i q", i=4)).then_inc(s_pe1, 1)
                if u < UNITS:
                    q = u % 2
                    dve.wait_ge(s_e, u + 1)
                    if u >= 2:
                        dve.wait_ge(s_norm, u - 1)
                    own.next(dve.tensor_tensor(sm["den"][:, q, :], sm["sum"][:, q, :], sm["sink"][:, q, :], ALU.add))
                    own.wait()
                    own.next(dve.reciprocal(sm["rden"][:, q, :], sm["den"][:, q, :]))
                    own.wait()
                    for i in range(4):
                        ins = dve.tensor_scalar(logit[:, q, i, :], logit[:, q, i, :], sm["rden"][:, q, i:i + 1], None,
                                                ALU.mult)
                        if i == 3:
                            ins.then_inc(s_norm, 1)
                        else:
                            own.next(ins)
                if u >= 2:
                    v = u - 2
                    jj, n = v // NT, v % NT
                    dve.wait_ge(s_pv, v + 1)
                    dve.tensor_scalar(bT[:, 2 * jj:2 * jj + 2, n * P:(n + 1) * P],
                                      ps[:, 6 + v % 2, 0:256].rearrange("p (a q) -> p a q", a=2), 0.5, None,
                                      ALU.mult).then_inc(s_ob, 1)
                if u < UNITS and u % 2:
                    g = u // 2
                    j, b = g // 2, g % 2
                    dve.wait_ge(z_th, g + 1)
                    if j >= 3:
                        dve.wait_ge(s_bg, j - 2)
                    dve.scalar_tensor_tensor(zg[:, (j + 1) % 3, HALF * b:HALF * (b + 1)], zt[:, :], 1.0, ps[:, g % 2, :],
                                             ALU.add, ALU.mult).then_inc(z_t, 1)
                if u == UNITS:
                    low_out(1, 0)
                    low_wo(1, 0)
            out_stage(1)


_INS = ["x", "a_w_in", "a_conv", "a_a_log", "a_dt_bias", "a_norm_g", "a_w_out", "b_w_in", "b_sinks", "b_w_out",
        "ln_g", "ln_b"]


def rope_tables():
    half = HD // 2
    inv = np.float32(10000.0) ** (-np.arange(half, dtype=np.float32) / np.float32(half))
    ang = np.arange(SEQ, dtype=np.float32)[:, None] * inv[None, :]
    cos, sin = np.cos(ang), np.sin(ang)
    return (np.concatenate([cos, cos], axis=1).astype(np.float32),
            np.concatenate([-sin, sin], axis=1).astype(np.float32))


def kernel(**inputs):
    import concourse.bacc as _bacc
    from concourse.bass_utils import run_bass_kernel_spmd as _run

    nc = _bacc.Bacc("TRN2", target_bir_lowering=False, num_devices=1)
    cos, sin = rope_tables()
    named = [(n, np.ascontiguousarray(inputs[n])) for n in _INS] + [("rope_cos", cos), ("rope_sin", sin)]
    arrays, args = {}, []
    for name, a in named:
        arrays[f"in_{name}"] = a
        args.append(nc.dram_tensor(f"in_{name}", a.shape, mybir.dt.from_np(a.dtype), kind="ExternalInput").ap())
    args.append(nc.dram_tensor("out_0", (1, SEQ, DM), F32, kind="ExternalOutput").ap())
    hybrid_trunk(nc, *args)
    r = _run(nc, [arrays], core_ids=[0])
    return r.results[0]["out_0"]
```
